# Optimizing a Trainium2 kernel written in Bass

```python
import numpy as np
import jax
import jax.numpy as jnp
from jax import lax

D_MODEL = 1024
BATCH = 1
SEQ = 1024
DEPTH = 2

Q_BLOCK = 128
NEG_INF = -1e30
MLA_HEADS = 8
MLA_Q_LORA = 256
MLA_KV_LORA = 128
MLA_NOPE_DIM = 64
MLA_ROPE_DIM = 32
MLA_V_DIM = 64
MLA_QK_DIM = MLA_NOPE_DIM + MLA_ROPE_DIM
ROPE_THETA = 10000.0
CONV_CHANNELS = 512
CONV_WIDTH = 31
MIX0_IN = MLA_Q_LORA + MLA_KV_LORA + MLA_ROPE_DIM + 2 * CONV_CHANNELS
MIX0_OUT = MLA_HEADS * MLA_V_DIM + CONV_CHANNELS
NSA_HEADS = 16
NSA_KV_GROUPS = 2
NSA_HEADS_PER_GROUP = NSA_HEADS // NSA_KV_GROUPS
NSA_HEAD_DIM = 64
NSA_KV_WIDTH = NSA_KV_GROUPS * NSA_HEAD_DIM
NSA_IN = NSA_HEADS * NSA_HEAD_DIM + 6 * NSA_KV_WIDTH + 3 * NSA_HEADS
CMP_BLOCK = 32
CMP_STRIDE = 16
CMP_HIDDEN = 128
SLC_BLOCK = 64
SLC_TOP_N = 8
WINDOW = 256
FORCE_SCORE = 1e4
MOE_GROUPS = 4
MOE_EXPERTS_PER_GROUP = 8
MOE_EXPERTS = MOE_GROUPS * MOE_EXPERTS_PER_GROUP
MOE_TOP_K = 2
MOE_HIDDEN = 256
MOE_ROW_BLOCK = 128

kernel_name = "hybrid_mla_conformer_nsa_hmoe"

def rms_norm(x, g, eps=1e-6):
    xf = x.astype(jnp.float32)
    y = xf * lax.rsqrt(jnp.mean(xf * xf, axis=-1, keepdims=True) + eps)
    return (y * g.astype(jnp.float32)).astype(x.dtype)

def layer_norm(x, g, b, eps=1e-5):
    xf = x.astype(jnp.float32)
    mu = jnp.mean(xf, axis=-1, keepdims=True)
    xc = xf - mu
    var = jnp.mean(xc * xc, axis=-1, keepdims=True)
    y = xc * lax.rsqrt(var + eps) * g.astype(jnp.float32) + b.astype(jnp.float32)
    return y.astype(x.dtype)

def alibi_slopes(n_heads):
    return jnp.asarray(2.0 ** (-8.0 * np.arange(1, n_heads + 1) / n_heads), jnp.float32)

def apply_rope(x, pos):
    half = x.shape[-1] // 2
    inv_freq = ROPE_THETA ** (-jnp.arange(half, dtype=jnp.float32) / half)
    ang = pos.astype(jnp.float32)[:, :, None, None] * inv_freq
    cos = jnp.cos(ang).astype(x.dtype)
    sin = jnp.sin(ang).astype(x.dtype)
    x1, x2 = x[..., :half], x[..., half:]
    return jnp.concatenate([x1 * cos - x2 * sin, x1 * sin + x2 * cos], axis=-1)

def causal_block_attention(q, k, v, scale):
    S = q.shape[2]
    outs = []
    for i in range(S // Q_BLOCK):
        end = (i + 1) * Q_BLOCK
        s = jnp.einsum('bhqd,bhkd->bhqk', q[:, :, i * Q_BLOCK:end], k[:, :, :end]).astype(jnp.float32) * scale
        mask = (i * Q_BLOCK + jnp.arange(Q_BLOCK))[:, None] >= jnp.arange(end)[None, :]
        p = jax.nn.softmax(jnp.where(mask, s, NEG_INF), axis=-1).astype(v.dtype)
        outs.append(jnp.einsum('bhqk,bhkd->bhqd', p, v[:, :, :end]))
    return jnp.concatenate(outs, axis=2)

def causal_depthwise_conv(u, w, b):
    C = u.shape[-1]
    y = lax.conv_general_dilated(u, w[:, None, :].astype(u.dtype), window_strides=(1,),
                                 padding=((CONV_WIDTH - 1, 0),),
                                 dimension_numbers=('NWC', 'WIO', 'NWC'), feature_group_count=C)
    return y + b

def mla_conv_mixer(h, pos, w_in, q_a_norm, w_uq, kv_a_norm, w_ukv, q_norm, k_norm,
                   dw_w, dw_b, ln_g, ln_b, w_out):
    B, S, _ = h.shape
    proj = h @ w_in
    c_q, c_kv, k_rope, conv_in = jnp.split(
        proj, [MLA_Q_LORA, MLA_Q_LORA + MLA_KV_LORA, MLA_Q_LORA + MLA_KV_LORA + MLA_ROPE_DIM], axis=-1)
    q = (rms_norm(c_q, q_a_norm) @ w_uq).reshape(B, S, MLA_HEADS, MLA_QK_DIM)
    kv = (rms_norm(c_kv, kv_a_norm) @ w_ukv).reshape(B, S, MLA_HEADS, MLA_NOPE_DIM + MLA_V_DIM)
    k_nope, v = kv[..., :MLA_NOPE_DIM], kv[..., MLA_NOPE_DIM:]
    k = jnp.concatenate(
        [k_nope, jnp.broadcast_to(k_rope[:, :, None, :], (B, S, MLA_HEADS, MLA_ROPE_DIM))], axis=-1)
    q = rms_norm(q, q_norm)
    k = rms_norm(k, k_norm)
    q = jnp.concatenate([q[..., :MLA_NOPE_DIM], apply_rope(q[..., MLA_NOPE_DIM:], pos)], axis=-1)
    k = jnp.concatenate([k[..., :MLA_NOPE_DIM], apply_rope(k[..., MLA_NOPE_DIM:], pos)], axis=-1)
    o_mla = causal_block_attention(q.transpose(0, 2, 1, 3), k.transpose(0, 2, 1, 3),
                                   v.transpose(0, 2, 1, 3), MLA_QK_DIM ** -0.5)
    o_mla = o_mla.transpose(0, 2, 1, 3).reshape(B, S, MLA_HEADS * MLA_V_DIM)
    a, g = jnp.split(conv_in, 2, axis=-1)
    u = causal_depthwise_conv(a * jax.nn.sigmoid(g), dw_w, dw_b)
    u = jax.nn.silu(layer_norm(u, ln_g, ln_b))
    return jnp.concatenate([o_mla, u], axis=-1) @ w_out

def compress_blocks(kv, pe, w1, w2):
    B, G, S, DK = kv.shape
    n_cmp = (S - CMP_BLOCK) // CMP_STRIDE + 1
    idx = CMP_STRIDE * np.arange(n_cmp)[:, None] + np.arange(CMP_BLOCK)[None, :]
    blocks = (kv[:, :, idx] + pe).reshape(B, G, n_cmp, CMP_BLOCK * DK)
    return jax.nn.gelu(blocks @ w1) @ w2

def compressed_attention(q, k_cmp, v_cmp, pos, slopes):
    S = q.shape[3]
    n_cmp = k_cmp.shape[2]
    end_idx = np.arange(n_cmp) * CMP_STRIDE + CMP_BLOCK - 1
    s = jnp.einsum('bghtd,bgcd->bghtc', q, k_cmp).astype(jnp.float32) * NSA_HEAD_DIM ** -0.5
    dist = (pos[:, :, None] - pos[:, end_idx][:, None, :]).astype(jnp.float32)
    valid = np.arange(S)[:, None] >= end_idx[None, :]
    s = s - slopes[None, :, :, None, None] * dist[:, None, None]
    s = jnp.where(valid, s, NEG_INF)
    m = jnp.max(s, axis=-1, keepdims=True)
    p = jnp.where(valid, jnp.exp(s - m), 0.0)
    p = p / jnp.maximum(jnp.sum(p, axis=-1, keepdims=True), 1e-20)
    o = jnp.einsum('bghtc,bgcd->bghtd', p.astype(v_cmp.dtype), v_cmp)
    return o, p

def select_blocks(p_cmp, S):
    n_cmp = p_cmp.shape[-1]
    n_sel = S // SLC_BLOCK
    cmp_start = np.arange(n_cmp) * CMP_STRIDE
    slc_start = np.arange(n_sel) * SLC_BLOCK
    overlap = (cmp_start[:, None] < slc_start[None, :] + SLC_BLOCK) & (cmp_start[:, None] + CMP_BLOCK > slc_start[None, :])
    imp = jnp.einsum('bghtc,cj->bgtj', p_cmp, jnp.asarray(overlap, jnp.float32))
    cur = np.arange(S)[:, None] // SLC_BLOCK
    j = np.arange(n_sel)[None, :]
    forced = (j == 0) | (j == cur) | (j == cur - 1)
    imp = jnp.where(forced, FORCE_SCORE, jnp.where(j <= cur, imp, -1.0))
    _, sel = lax.top_k(imp, min(SLC_TOP_N, n_sel))
    return sel

def selected_attention(q, k, v, pos, sel, slopes):
    B, G, HPG, S, DK = q.shape
    n_sel = S // SLC_BLOCK
    nq = S // Q_BLOCK
    n_top = sel.shape[-1]
    kb = k.reshape(B, G, n_sel, SLC_BLOCK, DK)
    vb = v.reshape(B, G, n_sel, SLC_BLOCK, DK)
    pos_blocks = pos.reshape(B, n_sel, SLC_BLOCK)
    q_c = q.reshape(B, G, HPG, nq, Q_BLOCK, DK).transpose(3, 0, 1, 2, 4, 5)
    sel_c = sel.reshape(B, G, nq, Q_BLOCK, n_top).transpose(2, 0, 1, 3, 4)
    pos_c = pos.reshape(B, nq, Q_BLOCK).transpose(1, 0, 2)
    starts = jnp.arange(nq, dtype=jnp.int32) * Q_BLOCK
    gather_kv = jax.vmap(jax.vmap(lambda blk, idx: blk[idx]))
    gather_pos = jax.vmap(lambda pb, idx: pb[idx])

    def one_block(args):
        qc, sc, pq, t0 = args
        kg = gather_kv(kb, sc)
        vg = gather_kv(vb, sc)
        pk = gather_pos(pos_blocks, sc)
        s = jnp.einsum('bghqd,bgqnld->bghqnl', qc, kg).astype(jnp.float32) * DK ** -0.5
        t_idx = t0 + jnp.arange(Q_BLOCK)
        k_idx = sc[..., None] * SLC_BLOCK + jnp.arange(SLC_BLOCK)
        valid = k_idx <= t_idx[None, None, :, None, None]
        dist = (pq[:, None, :, None, None] - pk).astype(jnp.float32)
        s = s - slopes[None, :, :, None, None, None] * dist[:, :, None]
        s = jnp.where(valid[:, :, None], s, NEG_INF).reshape(B, G, HPG, Q_BLOCK, n_top * SLC_BLOCK)
        p = jax.nn.softmax(s, axis=-1).reshape(B, G, HPG, Q_BLOCK, n_top, SLC_BLOCK).astype(v.dtype)
        return jnp.einsum('bghqnl,bgqnld->bghqd', p, vg)

    o = lax.map(one_block, (q_c, sel_c, pos_c, starts))
    return o.transpose(1, 2, 3, 0, 4, 5).reshape(B, G, HPG, S, DK)

def window_attention(q, k, v, pos, slopes):
    B, G, HPG, S, DK = q.shape
    nq = S // Q_BLOCK
    span = WINDOW + Q_BLOCK
    k_pad = jnp.pad(k, ((0, 0), (0, 0), (WINDOW, 0), (0, 0)))
    v_pad = jnp.pad(v, ((0, 0), (0, 0), (WINDOW, 0), (0, 0)))
    pos_pad = jnp.pad(pos, ((0, 0), (WINDOW, 0)))
    q_c = q.reshape(B, G, HPG, nq, Q_BLOCK, DK).transpose(3, 0, 1, 2, 4, 5)
    pos_c = pos.reshape(B, nq, Q_BLOCK).transpose(1, 0, 2)
    starts = jnp.arange(nq, dtype=jnp.int32) * Q_BLOCK

    def one_block(args):
        qc, pq, t0 = args
        kb = lax.dynamic_slice_in_dim(k_pad, t0, span, axis=2)
        vb = lax.dynamic_slice_in_dim(v_pad, t0, span, axis=2)
        pk = lax.dynamic_slice_in_dim(pos_pad, t0, span, axis=1)
        s = jnp.einsum('bghqd,bgkd->bghqk', qc, kb).astype(jnp.float32) * DK ** -0.5
        t_idx = t0 + jnp.arange(Q_BLOCK)
        k_idx = t0 - WINDOW + jnp.arange(span)
        rel = t_idx[:, None] - k_idx[None, :]
        valid = (k_idx[None, :] >= 0) & (rel >= 0) & (rel < WINDOW)
        dist = (pq[:, :, None] - pk[:, None, :]).astype(jnp.float32)
        s = s - slopes[None, :, :, None, None] * dist[:, None, None]
        p = jax.nn.softmax(jnp.where(valid, s, NEG_INF), axis=-1).astype(v.dtype)
        return jnp.einsum('bghqk,bgkd->bghqd', p, vb)

    o = lax.map(one_block, (q_c, pos_c, starts))
    return o.transpose(1, 2, 3, 0, 4, 5).reshape(B, G, HPG, S, DK)

def nsa_mixer(h, pos, slopes, w_in, q_norm, k_norm_cmp, k_norm_slc, k_norm_win,
              cmp_pe_k, cmp_w1_k, cmp_w2_k, cmp_pe_v, cmp_w1_v, cmp_w2_v, w_out):
    B, S, _ = h.shape
    G, HPG, DK = NSA_KV_GROUPS, NSA_HEADS_PER_GROUP, NSA_HEAD_DIM
    proj = h @ w_in
    split_pts = np.cumsum([NSA_HEADS * DK] + [NSA_KV_WIDTH] * 6).tolist()
    q, kc, vc, ks, vs, kw, vw, gates = jnp.split(proj, split_pts, axis=-1)
    q = rms_norm(q.reshape(B, S, G, HPG, DK), q_norm).transpose(0, 2, 3, 1, 4)
    to_kv = lambda t: t.reshape(B, S, G, DK).transpose(0, 2, 1, 3)
    k_cmp = rms_norm(compress_blocks(to_kv(kc), cmp_pe_k, cmp_w1_k, cmp_w2_k), k_norm_cmp)
    v_cmp = compress_blocks(to_kv(vc), cmp_pe_v, cmp_w1_v, cmp_w2_v)
    o_cmp, p_cmp = compressed_attention(q, k_cmp, v_cmp, pos, slopes)
    sel = select_blocks(p_cmp, S)
    o_slc = selected_attention(q, rms_norm(to_kv(ks), k_norm_slc), to_kv(vs), pos, sel, slopes)
    o_win = window_attention(q, rms_norm(to_kv(kw), k_norm_win), to_kv(vw), pos, slopes)
    g = jax.nn.sigmoid(gates).reshape(B, S, 3, G, HPG).transpose(2, 0, 3, 4, 1)[..., None]
    o = g[0] * o_cmp + g[1] * o_slc + g[2] * o_win
    return o.transpose(0, 3, 1, 2, 4).reshape(B, S, NSA_HEADS * DK) @ w_out

def hierarchical_moe(h, router_group, router_group_b, router_expert, router_expert_b, w_gate, w_up, w_down):
    B, S, D = h.shape
    T = B * S
    xt = h.reshape(T, D)
    g_logits = (xt @ router_group).astype(jnp.float32) + router_group_b.astype(jnp.float32)
    _, grp = lax.top_k(g_logits, 1)
    g_w = jnp.take_along_axis(jax.nn.softmax(g_logits, axis=-1), grp, axis=-1)
    e_logits = ((xt @ router_expert).astype(jnp.float32) + router_expert_b.astype(jnp.float32)
                ).reshape(T, MOE_GROUPS, MOE_EXPERTS_PER_GROUP)
    e_in = jnp.take_along_axis(e_logits, grp[:, :, None], axis=1)[:, 0]
    top_val, top_idx = lax.top_k(e_in, MOE_TOP_K)
    gates = jax.nn.softmax(top_val, axis=-1) * g_w
    expert = grp * MOE_EXPERTS_PER_GROUP + top_idx
    A = T * MOE_TOP_K
    e_flat = expert.reshape(A)
    tok_flat = jnp.repeat(jnp.arange(T, dtype=jnp.int32), MOE_TOP_K)
    w_flat = gates.reshape(A).astype(h.dtype)
    order = jnp.argsort(e_flat)
    e_sorted = e_flat[order]
    counts = jnp.bincount(e_flat, length=MOE_EXPERTS)
    starts = jnp.cumsum(counts) - counts
    padded = (counts + MOE_ROW_BLOCK - 1) // MOE_ROW_BLOCK * MOE_ROW_BLOCK
    padded_end = jnp.cumsum(padded)
    dest = (padded_end - padded)[e_sorted] + (jnp.arange(A) - starts[e_sorted])
    R = A + MOE_EXPERTS * MOE_ROW_BLOCK
    n_blk = R // MOE_ROW_BLOCK
    row_tok = jnp.full((R,), T, jnp.int32).at[dest].set(tok_flat[order])
    row_w = jnp.zeros((R,), h.dtype).at[dest].set(w_flat[order])
    blk_expert = jnp.clip(jnp.searchsorted(padded_end, jnp.arange(n_blk) * MOE_ROW_BLOCK, side='right'),
                          0, MOE_EXPERTS - 1)
    x_pad = jnp.concatenate([xt, jnp.zeros((1, D), xt.dtype)], axis=0)

    def expert_block(args):
        toks, wts, e = args
        rows = x_pad[toks]
        y = (jax.nn.silu(rows @ w_gate[e]) * (rows @ w_up[e])) @ w_down[e]
        return y * wts[:, None]

    ys = lax.map(expert_block, (row_tok.reshape(n_blk, MOE_ROW_BLOCK), row_w.reshape(n_blk, MOE_ROW_BLOCK), blk_expert))
    out = jax.ops.segment_sum(ys.reshape(R, D), row_tok, num_segments=T + 1)[:T]
    return out.reshape(B, S, D).astype(h.dtype)

def setup_inputs(seed: int = 0) -> dict:
    key = jax.random.key(seed)
    keys = iter(jax.random.split(key, 64))
    n_even = (DEPTH + 1) // 2
    n_odd = DEPTH // 2
    D = D_MODEL

    def dense(shape, fan_in):
        return jax.random.normal(next(keys), shape, jnp.float32) * fan_in ** -0.5

    def gain(shape):
        return 1.0 + 0.05 * jax.random.normal(next(keys), shape, jnp.float32)

    def small(shape, scale=0.02):
        return scale * jax.random.normal(next(keys), shape, jnp.float32)

    x = jax.random.normal(next(keys), (BATCH, SEQ, D), jnp.float32)
    positions = (jnp.cumsum(jax.random.randint(next(keys), (BATCH, SEQ), 1, 3), axis=1) - 1).astype(jnp.int32)
    L, DK = CMP_BLOCK, NSA_HEAD_DIM
    return {
        "x": x,
        "positions": positions,
        "norm_mix": gain((DEPTH, D)),
        "norm_ffn": gain((DEPTH, D)),
        "mix0_w_in": dense((n_even, D, MIX0_IN), D),
        "mla_q_a_norm": gain((n_even, MLA_Q_LORA)),
        "mla_w_uq": dense((n_even, MLA_Q_LORA, MLA_HEADS * MLA_QK_DIM), MLA_Q_LORA),
        "mla_kv_a_norm": gain((n_even, MLA_KV_LORA)),
        "mla_w_ukv": dense((n_even, MLA_KV_LORA, MLA_HEADS * (MLA_NOPE_DIM + MLA_V_DIM)), MLA_KV_LORA),
        "mla_q_norm": gain((n_even, MLA_QK_DIM)),
        "mla_k_norm": gain((n_even, MLA_QK_DIM)),
        "conv_dw_w": dense((n_even, CONV_WIDTH, CONV_CHANNELS), CONV_WIDTH),
        "conv_dw_b": small((n_even, CONV_CHANNELS)),
        "conv_ln_g": gain((n_even, CONV_CHANNELS)),
        "conv_ln_b": small((n_even, CONV_CHANNELS)),
        "mix0_w_out": dense((n_even, MIX0_OUT, D), MIX0_OUT),
        "nsa_w_in": dense((n_odd, D, NSA_IN), D),
        "nsa_q_norm": gain((n_odd, DK)),
        "nsa_k_norm_cmp": gain((n_odd, DK)),
        "nsa_k_norm_slc": gain((n_odd, DK)),
        "nsa_k_norm_win": gain((n_odd, DK)),
        "nsa_cmp_pe_k": small((n_odd, L, DK), 0.1),
        "nsa_cmp_w1_k": dense((n_odd, L * DK, CMP_HIDDEN), L * DK),
        "nsa_cmp_w2_k": dense((n_odd, CMP_HIDDEN, DK), CMP_HIDDEN),
        "nsa_cmp_pe_v": small((n_odd, L, DK), 0.1),
        "nsa_cmp_w1_v": dense((n_odd, L * DK, CMP_HIDDEN), L * DK),
        "nsa_cmp_w2_v": dense((n_odd, CMP_HIDDEN, DK), CMP_HIDDEN),
        "nsa_w_out": dense((n_odd, NSA_HEADS * DK, D), NSA_HEADS * DK),
        "moe_router_group": dense((DEPTH, D, MOE_GROUPS), D),
        "moe_router_group_b": small((DEPTH, MOE_GROUPS), 0.01),
        "moe_router_expert": dense((DEPTH, D, MOE_EXPERTS), D),
        "moe_router_expert_b": small((DEPTH, MOE_EXPERTS), 0.01),
        "moe_w_gate": dense((DEPTH, MOE_EXPERTS, D, MOE_HIDDEN), D),
        "moe_w_up": dense((DEPTH, MOE_EXPERTS, D, MOE_HIDDEN), D),
        "moe_w_down": dense((DEPTH, MOE_EXPERTS, MOE_HIDDEN, D), MOE_HIDDEN),
    }

def reference(x, positions, norm_mix, norm_ffn, mix0_w_in, mla_q_a_norm, mla_w_uq, mla_kv_a_norm,
              mla_w_ukv, mla_q_norm, mla_k_norm, conv_dw_w, conv_dw_b, conv_ln_g, conv_ln_b, mix0_w_out,
              nsa_w_in, nsa_q_norm, nsa_k_norm_cmp, nsa_k_norm_slc, nsa_k_norm_win,
              nsa_cmp_pe_k, nsa_cmp_w1_k, nsa_cmp_w2_k, nsa_cmp_pe_v, nsa_cmp_w1_v, nsa_cmp_w2_v, nsa_w_out,
              moe_router_group, moe_router_group_b, moe_router_expert, moe_router_expert_b,
              moe_w_gate, moe_w_up, moe_w_down):
    slopes = alibi_slopes(NSA_HEADS).reshape(NSA_KV_GROUPS, NSA_HEADS_PER_GROUP)
    for layer in range(DEPTH):
        i = layer // 2
        h = rms_norm(x, norm_mix[layer])
        if layer % 2 == 0:
            mix = mla_conv_mixer(h, positions, mix0_w_in[i], mla_q_a_norm[i], mla_w_uq[i], mla_kv_a_norm[i],
                                 mla_w_ukv[i], mla_q_norm[i], mla_k_norm[i], conv_dw_w[i], conv_dw_b[i],
                                 conv_ln_g[i], conv_ln_b[i], mix0_w_out[i])
        else:
            mix = nsa_mixer(h, positions, slopes, nsa_w_in[i], nsa_q_norm[i], nsa_k_norm_cmp[i],
                            nsa_k_norm_slc[i], nsa_k_norm_win[i], nsa_cmp_pe_k[i], nsa_cmp_w1_k[i],
                            nsa_cmp_w2_k[i], nsa_cmp_pe_v[i], nsa_cmp_w1_v[i], nsa_cmp_w2_v[i], nsa_w_out[i])
        x = x + mix
        x = x + hierarchical_moe(rms_norm(x, norm_ffn[layer]), moe_router_group[layer], moe_router_group_b[layer],
                                 moe_router_expert[layer], moe_router_expert_b[layer],
                                 moe_w_gate[layer], moe_w_up[layer], moe_w_down[layer])
    return x


_drawn_inputs = setup_inputs


def setup_inputs(seed=0):
    import zlib

    import numpy as np

    out = dict(_drawn_inputs(seed))
    spreads = {}
    factors = {'mla_q_norm': 2.776,
     'mla_k_norm': 2.735,
     'nsa_q_norm': 3.48,
     'nsa_k_norm_cmp': 6.223,
     'nsa_k_norm_slc': 4.443,
     'nsa_k_norm_win': 4.195,
     'nsa_cmp_pe_k': 4.115,
     'moe_router_group_b': 2.784,
     'moe_router_expert_b': 4.137}
    for name, (base, spread) in spreads.items():
        noise = np.random.default_rng([zlib.crc32(name.encode()), seed]).standard_normal(out[name].shape)
        drawn = base * np.exp(spread * noise) if base else spread * noise
        out[name] = jnp.asarray(drawn.astype(out[name].dtype))
    for name, factor in factors.items():
        out[name] = (out[name] * factor).astype(out[name].dtype)
    return out
```

```python
from contextlib import ExitStack

import numpy as np
import concourse.bass as bass
from concourse import mybir

F32 = mybir.dt.float32
I32 = mybir.dt.int32
U32 = mybir.dt.uint32
ALU = mybir.AluOpType
ACT = mybir.ActivationFunctionType
X_AXIS = mybir.AxisListType.X

P = 128
SEQ = 1024
TILES = SEQ // P
D = 1024
CHUNKS = D // P
BANK = 512
RMS_EPS = 1e-6
LN_EPS = 1e-5
BIG = 1e30

MLA_HEADS = 8
Q_LORA = 256
KV_LORA = 128
NOPE = 64
ROPE = 32
HALF = ROPE // 2
V_DIM = 64
QK = NOPE + ROPE
LATENT = Q_LORA + KV_LORA + ROPE
CONV = 512
CONV_TILES = CONV // P
TAPS = 31
MIX0_IN = LATENT + 2 * CONV
ROPE_THETA = 10000.0


class Phase:

    numbers = []

    def __init__(self, nc, name):
        self.nc, self.name, self.stack = nc, name, ExitStack()

    def __enter__(self):
        self.stack.__enter__()
        return self

    def __exit__(self, *a):
        return self.stack.__exit__(*a)

    def sb(self, name, shape, dt=F32):
        return self.stack.enter_context(self.nc.sbuf_tensor(f"{self.name}_{name}", shape, dt))

    def ps(self, name, shape=(P, BANK)):
        return self.stack.enter_context(self.nc.psum_tensor(f"{self.name}_{name}", list(shape), F32))

    def sem(self, name):
        s = self.stack.enter_context(self.nc.semaphore(f"{self.name}_{name}"))
        Phase.numbers.append(s.num)
        return s


def clear_semaphores(nc):
    numbers = sorted(set(Phase.numbers))
    ends = [n for n in numbers if n + 1 not in numbers]
    for first, last in zip([n for n in numbers if n - 1 not in numbers], ends):
        nc.gpsimd.sem_clear(range(first, last + 1))
    Phase.numbers.clear()
    nc.all_engine_barrier()


class Own:

    def __init__(self, eng, sem):
        self.eng, self.sem, self.n = eng, sem, 0

    def link(self, ins):
        self.n += 1
        ins.then_inc(self.sem, 1)
        self.eng.wait_ge(self.sem, self.n)


def over(ap, shape):
    return ap.broadcast_to(list(shape))


def constants(nc, x_rows, ident, ones, A):
    with Phase(nc, "const") as ph:
        x_here, zeroed, ready = ph.sem("x_here"), ph.sem("zeroed"), ph.sem("ready")
        x_dram = A["x"].rearrange("b (t p) d -> p (b t) d", p=P)
        with nc.Block() as block:
            @block.sync
            def _(sp):
                for t in range(TILES):
                    sp.dma_start(x_rows[:, t, :], x_dram[:, t, :]).then_inc(x_here, 16)
                sp.wait_ge(x_here, 16 * TILES)

            @block.gpsimd
            def _(pool):
                pool.memset(ident[:, :], 0.0).then_inc(zeroed, 1)
                pool.memset(ones[:, :], 1.0).then_inc(ready, 1)
                pool.wait_ge(zeroed, 1)
                pool.affine_select(out=ident[:, :], in_=ident[:, :], compare_op=ALU.not_equal, fill=1.0,
                                   base=0, pattern=[[-1, P]], channel_multiplier=1).then_inc(ready, 1)


def norm_columns(nc, name, x_rows, gain_row, ident, h_cols, h_dram=None):
    with Phase(nc, name) as ph:
        gain = ph.sb("gain", [P, D])
        square = ph.sb("square", [P, 2, D])
        total = ph.sb("total", [P, TILES])
        mean = ph.sb("mean", [P, TILES])
        inv = ph.sb("inv", [P, TILES])
        rstd = ph.sb("rstd", [P, TILES])
        h_rows = ph.sb("h_rows", [P, 3, D])
        turn = [ph.ps(f"turn{i}") for i in range(8)]
        gain_here, summed, own, rstd_ready = ph.sem("gain"), ph.sem("summed"), ph.sem("own"), ph.sem("rstd")
        rows_ready, turned, copied_act, copied_dve = (
            ph.sem(n) for n in ("rows", "turned", "copied_act", "copied_dve"))
        stored = [ph.sem(f"stored{i}") for i in range(3)]
        GROUPS = 2

        def bank(t, g):
            return turn[(t * GROUPS + g) % 8]

        with nc.Block() as block:
            @block.sync
            def _(sp):
                sp.dma_start(gain[:, :], gain_row.partition_broadcast(P)).then_inc(gain_here, 16)
                if h_dram is not None:
                    for t in range(TILES):
                        sp.wait_ge(rows_ready, t + 1)
                        sp.dma_start(h_dram[t * P:(t + 1) * P, :], h_rows[:, t % 3, :]).then_inc(stored[t % 3], 16)
                    for b in range(3):
                        sp.wait_ge(stored[b], 16 * len(range(b, TILES, 3)))

            @block.scalar
            def _(act):
                for t in range(TILES):
                    if t >= 2:
                        act.wait_ge(summed, t - 1)
                    act.activation(square[:, t % 2, :], x_rows[:, t, :], ACT.Square,
                                   accum_out=total[:, t:t + 1]).then_inc(summed, 1)
                act.wait_ge(own, 2)
                act.activation(rstd[:, :], inv[:, :], ACT.Sqrt).then_inc(rstd_ready, 1)
                for t in range(TILES):
                    act.wait_ge(turned, GROUPS * t + 1)
                    act.activation(h_cols[:, 0:4, t * P:(t + 1) * P],
                                   bank(t, 0).rearrange("p (c n) -> p c n", c=4), ACT.Copy).then_inc(copied_act, 1)

            def copy_half(dve, t):
                dve.wait_ge(turned, GROUPS * t + 2)
                dve.tensor_copy(h_cols[:, 4:8, t * P:(t + 1) * P],
                                bank(t, 1).rearrange("p (c n) -> p c n", c=4)).then_inc(copied_dve, 1)

            @block.vector
            def _(dve):
                mine = Own(dve, own)
                dve.wait_ge(summed, TILES)
                mine.link(dve.tensor_scalar(mean[:, :], total[:, :], 1.0 / D, RMS_EPS, ALU.mult, ALU.add))
                mine.link(dve.reciprocal(inv[:, :], mean[:, :]))
                dve.wait_ge(rstd_ready, 1)
                dve.wait_ge(gain_here, 16)
                for t in range(TILES):
                    if t >= 3:
                        dve.wait_ge(turned, GROUPS * (t - 2))
                        if h_dram is not None:
                            dve.wait_ge(stored[t % 3], 16 * (t // 3))
                    dve.scalar_tensor_tensor(out=h_rows[:, t % 3, :], in0=x_rows[:, t, :], scalar=rstd[:, t:t + 1],
                                             in1=gain[:, :], op0=ALU.mult, op1=ALU.mult).then_inc(rows_ready, 1)
                    if t >= 1:
                        copy_half(dve, t - 1)
                copy_half(dve, TILES - 1)

            @block.tensor
            def _(pe):
                for t in range(TILES):
                    pe.wait_ge(rows_ready, t + 1)
                    spread = h_rows[:, t % 3, :].rearrange("n (p c) -> n c p", c=CHUNKS)
                    for g in range(GROUPS):
                        if t >= 4:
                            pe.wait_ge(copied_dve if g else copied_act, t - 3)
                        for j in range(4):
                            last = pe.transpose(bank(t, g)[:, j * P:(j + 1) * P], spread[:, 4 * g + j, :], ident[:, :])
                        last.then_inc(turned, 1)


def store_rows(nc, x_rows, out):
    with Phase(nc, "store") as ph:
        stored = ph.sem("stored")
        o = out.rearrange("b (t p) d -> p (b t) d", p=P)
        with nc.Block() as block:
            @block.sync
            def _(sp):
                for t in range(TILES):
                    sp.dma_start(o[:, t, :], x_rows[:, t, :]).then_inc(stored, 16)
                sp.wait_ge(stored, 16 * TILES)


def mix0_input(nc, h_cols, w_in, w_in_here, latents, conv_out, A):
    HALVES = SEQ // BANK
    UNITS = CONV_TILES * HALVES
    PAD = TAPS - 1
    with Phase(nc, "mix0in") as ph:
        gated = ph.sb("gated", [P, CONV_TILES, PAD + SEQ])
        sig = ph.sb("sig", [P, 2, BANK])
        odd = ph.sb("odd", [P, SEQ])
        taps = ph.sb("taps", [P, CONV_TILES, TAPS])
        bias = ph.sb("bias", [P, CONV_TILES])
        val = [ph.ps(f"val{i}") for i in range(3)]
        gate = [ph.ps(f"gate{i}") for i in range(3)]
        lat = [ph.ps(f"lat{i}") for i in range(2)]
        small_here, padded, projected, sig_ready, glu_ready, tapped = (
            ph.sem(n) for n in ("small", "padded", "projected", "sig", "glu", "tapped"))
        lat_done, lat_copied = ph.sem("lat_done"), ph.sem("lat_copied")

        with nc.Block() as block:
            @block.sync
            def _(sp):
                with nc.allow_non_contiguous_dma(reason="small weights, once"):
                    for ct in range(CONV_TILES):
                        sp.dma_start(taps[:, ct, :], A["conv_dw_w"][0, :, ct * P:(ct + 1) * P].rearrange(
                            "j p -> p j")).then_inc(small_here, 16)
                    sp.dma_start(bias[:, :], A["conv_dw_b"][0].rearrange("(c p) -> p c", p=P)).then_inc(small_here, 16)

            @block.tensor
            def _(pe):
                pe.wait_ge(w_in_here, 16)
                for u in range(UNITS):
                    ct, half = u // HALVES, u % HALVES
                    if u >= 3:
                        pe.wait_ge(glu_ready, u - 2)
                    for to, first in ((val[u % 3], LATENT), (gate[u % 3], LATENT + CONV)):
                        for c in range(CHUNKS):
                            last = pe.matmul(to[:, :], w_in[:, c, first + ct * P:first + (ct + 1) * P],
                                             h_cols[:, c, half * BANK:(half + 1) * BANK],
                                             start=(c == 0), stop=(c == CHUNKS - 1))
                    last.then_inc(projected, 1)
                for t in range(TILES):
                    if t >= 2:
                        pe.wait_ge(lat_copied, t - 1)
                    for c in range(CHUNKS):
                        last = pe.matmul(lat[t % 2][:, 0:LATENT], h_cols[:, c, t * P:(t + 1) * P],
                                         w_in[:, c, 0:LATENT], start=(c == 0), stop=(c == CHUNKS - 1))
                    last.then_inc(lat_done, 1)

            @block.scalar
            def _(act):
                for u in range(UNITS):
                    act.wait_ge(projected, u + 1)
                    if u >= 2:
                        act.wait_ge(glu_ready, u - 1)
                    act.activation(sig[:, u % 2, :], gate[u % 3][:, :], ACT.Sigmoid).then_inc(sig_ready, 1)
                for t in range(TILES):
                    act.wait_ge(lat_done, t + 1)
                    act.activation(latents[:, t, :], lat[t % 2][:, 0:LATENT], ACT.Copy).then_inc(lat_copied, 1)

            @block.vector
            def _(dve):
                dve.memset(gated[:, :, 0:PAD], 0.0).then_inc(padded, 1)

                def glu(u):
                    ct, half = u // HALVES, u % HALVES
                    dve.wait_ge(sig_ready, u + 1)
                    dve.tensor_tensor(gated[:, ct, PAD + half * BANK:PAD + (half + 1) * BANK],
                                      val[u % 3][:, :], sig[:, u % 2, :], ALU.mult).then_inc(glu_ready, 1)

                done = 0
                glu(0)
                glu(1)
                dve.wait_ge(padded, 1)
                dve.wait_ge(small_here, 16 * (CONV_TILES + 1))
                for ct in range(CONV_TILES):
                    dve.wait_ge(glu_ready, HALVES * (ct + 1))
                    for j in range(TAPS):
                        to = odd[:, :] if j % 2 else conv_out[:, ct, :]
                        shifted, w = gated[:, ct, j:j + SEQ], taps[:, ct, j:j + 1]
                        if j == 0:
                            ins = dve.tensor_scalar(to, shifted, w, bias[:, ct:ct + 1], ALU.mult, ALU.add)
                        elif j == 1:
                            if ct:
                                dve.wait_ge(tapped, done - 1)
                            ins = dve.tensor_scalar(to, shifted, w, None, ALU.mult)
                        else:
                            dve.wait_ge(tapped, done - 1)
                            ins = dve.scalar_tensor_tensor(out=to, in0=shifted, scalar=w, in1=to,
                                                           op0=ALU.mult, op1=ALU.add)
                        ins.then_inc(tapped, 1)
                        done += 1
                        if j in (12, 25) and ct + 1 < CONV_TILES:
                            glu(HALVES * (ct + 1) + (j == 25))
                    dve.wait_ge(tapped, done)
                    dve.tensor_tensor(conv_out[:, ct, :], conv_out[:, ct, :], odd[:, :], ALU.add).then_inc(tapped, 1)
                    done += 1


def conv_norm(nc, conv_out, ones, o_cols, A):
    HALVES = SEQ // BANK
    with Phase(nc, "convnorm") as ph:
        g = ph.sb("g", [P, CONV_TILES])
        b = ph.sb("b", [P, CONV_TILES])
        centred = ph.sb("centred", [P, CONV_TILES, SEQ])
        square = ph.sb("square", [P, CONV_TILES, SEQ])
        inv = ph.sb("inv", [P, SEQ])
        rstd = ph.sb("rstd", [P, SEQ])
        sums = [ph.ps(f"sums{i}") for i in range(HALVES)]
        squares = [ph.ps(f"squares{i}") for i in range(HALVES)]
        here, sum_ready, centre_ready, square_ready, own, rstd_ready, scaled, affine, sig_ready = (
            ph.sem(n) for n in ("here", "sum", "centre", "square", "own", "rstd", "scaled", "affine", "sig"))
        units = [(h, ct) for h in range(HALVES) for ct in range(CONV_TILES)]

        def part(h):
            return slice(h * BANK, (h + 1) * BANK)

        with nc.Block() as block:
            @block.sync
            def _(sp):
                with nc.allow_non_contiguous_dma(reason="small weights, once"):
                    sp.dma_start(g[:, :], A["conv_ln_g"][0].rearrange("(c p) -> p c", p=P)).then_inc(here, 16)
                    sp.dma_start(b[:, :], A["conv_ln_b"][0].rearrange("(c p) -> p c", p=P)).then_inc(here, 16)

            @block.tensor
            def _(pe):
                for h in range(HALVES):
                    for ct in range(CONV_TILES):
                        last = pe.matmul(sums[h][:, :], ones[:, :], conv_out[:, ct, part(h)],
                                         start=(ct == 0), stop=(ct == CONV_TILES - 1))
                    last.then_inc(sum_ready, 1)
                for n, (h, ct) in enumerate(units):
                    pe.wait_ge(square_ready, n + 1)
                    last = pe.matmul(squares[h][:, :], ones[:, :], square[:, ct, part(h)],
                                     start=(ct == 0), stop=(ct == CONV_TILES - 1))
                    if ct == CONV_TILES - 1:
                        last.then_inc(sum_ready, 1)

            @block.vector
            def _(dve):
                mine = Own(dve, own)
                for n, (h, ct) in enumerate(units):
                    dve.wait_ge(sum_ready, h + 1)
                    dve.scalar_tensor_tensor(out=centred[:, ct, part(h)], in0=sums[h][:, :], scalar=-1.0 / CONV,
                                             in1=conv_out[:, ct, part(h)], op0=ALU.mult, op1=ALU.add
                                             ).then_inc(centre_ready, 1)
                for h in range(HALVES):
                    dve.wait_ge(sum_ready, HALVES + h + 1)
                    mine.link(dve.tensor_scalar(inv[:, part(h)], squares[h][:, :], 1.0 / CONV, LN_EPS,
                                                ALU.mult, ALU.add))
                    mine.link(dve.reciprocal(inv[:, part(h)], inv[:, part(h)]))
                for n, (h, ct) in enumerate(units):
                    dve.wait_ge(rstd_ready, h + 1)
                    dve.tensor_tensor(centred[:, ct, part(h)], centred[:, ct, part(h)], rstd[:, part(h)],
                                      ALU.mult).then_inc(scaled, 1)
                for n, (h, ct) in enumerate(units):
                    dve.wait_ge(sig_ready, n + 1)
                    dve.tensor_tensor(o_cols[:, MLA_HEADS * V_DIM // P + ct, part(h)], centred[:, ct, part(h)],
                                      square[:, ct, part(h)], ALU.mult)

            @block.scalar
            def _(act):
                for n, (h, ct) in enumerate(units):
                    act.wait_ge(centre_ready, n + 1)
                    act.activation(square[:, ct, part(h)], centred[:, ct, part(h)], ACT.Square).then_inc(square_ready, 1)
                for h in range(HALVES):
                    act.wait_ge(own, 2 * (h + 1))
                    act.activation(rstd[:, part(h)], inv[:, part(h)], ACT.Sqrt).then_inc(rstd_ready, 1)
                act.wait_ge(here, 32)
                act.wait_ge(sum_ready, 2 * HALVES)
                for n, (h, ct) in enumerate(units):
                    act.wait_ge(scaled, n + 1)
                    act.activation(centred[:, ct, part(h)], centred[:, ct, part(h)], ACT.Identity,
                                   bias=b[:, ct:ct + 1], scale=g[:, ct:ct + 1]).then_inc(affine, 1)
                    act.wait_ge(affine, n + 1)
                    act.activation(square[:, ct, part(h)], centred[:, ct, part(h)], ACT.Sigmoid).then_inc(sig_ready, 1)


def project_out(nc, name, o_cols, w_view, x_rows):
    HALVES = D // BANK
    with Phase(nc, name) as ph:
        w = ph.sb("w", [P, HALVES, CHUNKS, BANK])
        acc = [ph.ps(f"acc{i}") for i in range(8)]
        w_here = [ph.sem(f"w{h}") for h in range(HALVES)]
        done, added = ph.sem("done"), ph.sem("added")
        with nc.Block() as block:
            @block.sync
            def _(sp):
                for h in range(HALVES):
                    sp.dma_start(w[:, h], w_view[:, :, h * BANK:(h + 1) * BANK]).then_inc(w_here[h], 16)

            @block.tensor
            def _(pe):
                for n in range(HALVES * TILES):
                    h, t = n // TILES, n % TILES
                    if t == 0:
                        pe.wait_ge(w_here[h], 16)
                    if n >= 8:
                        pe.wait_ge(added, n - 7)
                    for c in range(CHUNKS):
                        last = pe.matmul(acc[n % 8][:, :], o_cols[:, c, t * P:(t + 1) * P], w[:, h, c, :],
                                         start=(c == 0), stop=(c == CHUNKS - 1))
                    last.then_inc(done, 1)

            @block.vector
            def _(dve):
                for n in range(HALVES * TILES):
                    h, t = n // TILES, n % TILES
                    dve.wait_ge(done, n + 1)
                    part = x_rows[:, t, h * BANK:(h + 1) * BANK]
                    dve.tensor_tensor(part, acc[n % 8][:, :], part, ALU.add).then_inc(added, 1)


def mla_inputs(nc, latents, q_cols, k_cols, v_rows, ident, A):
    HEADS2 = 2 * MLA_HEADS
    UP = MLA_HEADS * QK
    with Phase(nc, "mlain") as ph:
        w_uq = ph.sb("w_uq", [P, 2, UP])
        w_ukv = ph.sb("w_ukv", [P, MLA_HEADS * (NOPE + V_DIM)])
        lat_gain = ph.sb("lat_gain", [P, Q_LORA + KV_LORA])
        qk_gain = ph.sb("qk_gain", [P, 2, QK])
        pos_i = ph.sb("pos_i", [P, TILES], I32)
        pos = ph.sb("pos", [P, TILES])
        freq = ph.sb("freq", [P, HALF])
        ang = ph.sb("ang", [P, TILES, HALF])
        turns = ph.sb("turns", [P, TILES, HALF])
        shifted = ph.sb("shifted", [P, TILES, HALF])
        sin = ph.sb("sin", [P, TILES, HALF])
        cos = ph.sb("cos", [P, TILES, HALF])
        junk = ph.sb("junk", [P, 2, Q_LORA])
        lat_sum = ph.sb("lat_sum", [P, 2, TILES])
        lat_rstd = ph.sb("lat_rstd", [P, 2, TILES])
        lat_n = ph.sb("lat_n", [P, 2, Q_LORA + KV_LORA])
        lat_cols = ph.sb("lat_cols", [P, 2, 3, P])
        qk = ph.sb("qk", [P, 2, HEADS2, QK])
        sq = ph.sb("sq", [P, 2, HEADS2, QK])
        ssum = ph.sb("ssum", [P, 2, HEADS2])
        rstd = ph.sb("rstd", [P, 2, HEADS2])
        q_up = ph.ps("q_up", (P, 2 * BANK))
        kv_up = ph.ps("kv_up", (P, 2 * BANK))
        lat_turn = ph.ps("lat_turn")
        turn = [ph.ps(f"turn{i}") for i in range(3)]
        (here, freq_set, own, lat_summed, lat_rstd_ready, lat_ready, lat_turned, lat_copied, up_done, qk_copied,
         rope_copied, squared, reduced, rstd_ready, qk_ready, turned, out_act, out_dve, angles, trig) = (ph.sem(n) for n in (
             "here", "freq", "own", "lat_summed", "lat_rstd", "lat_ready", "lat_turned", "lat_copied", "up",
             "qk_copied", "rope", "squared", "reduced", "rstd", "qk_ready", "turned", "out_act", "out_dve",
             "angles", "trig"))
        GROUPS = HEADS2 // 4

        with nc.Block() as block:
            @block.sync
            def _(sp):
                with nc.allow_non_contiguous_dma(reason="small, once"):
                    sp.dma_start(pos_i[:, :], A["positions"].rearrange("b (t p) -> p (b t)", p=P)).then_inc(here, 16)
                sp.dma_start(lat_gain[:, 0:Q_LORA], A["mla_q_a_norm"][0].partition_broadcast(P)).then_inc(here, 16)
                sp.dma_start(lat_gain[:, Q_LORA:], A["mla_kv_a_norm"][0].partition_broadcast(P)).then_inc(here, 16)
                sp.dma_start(qk_gain[:, 0, :], A["mla_q_norm"][0].partition_broadcast(P)).then_inc(here, 16)
                sp.dma_start(qk_gain[:, 1, :], A["mla_k_norm"][0].partition_broadcast(P)).then_inc(here, 16)
                sp.dma_start(w_uq[:, :, :], A["mla_w_uq"][0].rearrange("(c p) n -> p c n", p=P)).then_inc(here, 16)
                sp.dma_start(w_ukv[:, :], A["mla_w_ukv"][0]).then_inc(here, 16)
            HERE = 16 * 7

            @block.gpsimd
            def _(pool):
                for j in range(HALF):
                    pool.memset(freq[:, j:j + 1], float(ROPE_THETA ** (-j / HALF))).then_inc(freq_set, 1)
                for t in range(TILES):
                    if t >= 2:
                        pool.wait_ge(turned, GROUPS * (t - 1))
                    pool.tensor_copy(qk[:, t % 2, MLA_HEADS:, NOPE:],
                                     over(latents[:, t:t + 1, Q_LORA + KV_LORA:], (P, MLA_HEADS, ROPE))
                                     ).then_inc(rope_copied, 1)

            @block.tensor
            def _(pe):
                pe.wait_ge(here, HERE)

                def up(t):
                    pe.wait_ge(lat_ready, 2 * (t + 1))
                    if t:
                        pe.wait_ge(lat_copied, t)
                    for c in range(3):
                        last = pe.transpose(lat_turn[:, c * P:(c + 1) * P], lat_n[:, t % 2, c * P:(c + 1) * P], ident[:, :])
                    last.then_inc(lat_turned, 1)
                    pe.wait_ge(lat_copied, t + 1)
                    if t:
                        pe.wait_ge(qk_copied, 3 * t)
                    for lo, hi in ((0, BANK), (BANK, UP)):
                        for c in range(2):
                            pe.matmul(q_up[:, lo:hi], lat_cols[:, t % 2, c, :], w_uq[:, c, lo:hi], start=(c == 0), stop=(c == 1))
                    for h in range(2):
                        last = pe.matmul(kv_up[:, h * BANK:(h + 1) * BANK], lat_cols[:, t % 2, 2, :],
                                         w_ukv[:, h * BANK:(h + 1) * BANK], start=True, stop=True)
                    last.then_inc(up_done, 1)

                def columns(t):
                    pe.wait_ge(qk_ready, t + 1)
                    for g in range(GROUPS):
                        n = GROUPS * t + g
                        if n >= 3:
                            pe.wait_ge(out_dve if (n - 3) % 2 else out_act, (n - 3) // 2 + 1)
                        for j in range(4):
                            last = pe.transpose(turn[n % 3][0:QK, j * P:(j + 1) * P], qk[:, t % 2, 4 * g + j, :], ident[:, :])
                        last.then_inc(turned, 1)

                for t in range(TILES + 1):
                    if t < TILES:
                        up(t)
                    if t:
                        columns(t - 1)

            def head_columns(n):
                t, g = n // GROUPS, n % GROUPS
                to = q_cols if g < GROUPS // 2 else k_cols
                h = 4 * (g % (GROUPS // 2))
                return to[0:QK, h:h + 4, t * P:(t + 1) * P]

            @block.scalar
            def _(act):
                for t in range(TILES):
                    for part, (lo, hi) in enumerate(((0, Q_LORA), (Q_LORA, Q_LORA + KV_LORA))):
                        n = 2 * t + part
                        if n >= 2:
                            act.wait_ge(lat_summed, n - 1)
                        act.activation(junk[:, part, 0:hi - lo], latents[:, t, lo:hi], ACT.Square,
                                       accum_out=lat_sum[:, part, t:t + 1]).then_inc(lat_summed, 1)
                act.wait_ge(own, 3)
                act.activation(lat_rstd[:, :, :], lat_sum[:, :, :], ACT.Sqrt).then_inc(lat_rstd_ready, 1)

                def up(t):
                    act.wait_ge(lat_turned, t + 1)
                    if t >= 2:
                        act.wait_ge(up_done, t - 1)
                    act.activation(lat_cols[:, t % 2, :, :], lat_turn[:, 0:3 * P].rearrange("p (c n) -> p c n", c=3),
                                   ACT.Copy).then_inc(lat_copied, 1)
                    act.wait_ge(up_done, t + 1)
                    if t >= 2:
                        act.wait_ge(turned, GROUPS * (t - 1))
                    act.activation(qk[:, t % 2, 0:MLA_HEADS, :], q_up[:, 0:UP].rearrange("p (h d) -> p h d", d=QK),
                                   ACT.Copy).then_inc(qk_copied, 1)
                    kv = kv_up[:, :].rearrange("p (h d) -> p h d", d=NOPE + V_DIM)
                    act.activation(qk[:, t % 2, MLA_HEADS:, 0:NOPE], kv[:, :, 0:NOPE], ACT.Copy).then_inc(qk_copied, 1)
                    act.activation(v_rows[:, t, :].rearrange("p (h d) -> p h d", d=V_DIM), kv[:, :, NOPE:],
                                   ACT.Copy).then_inc(qk_copied, 1)
                    act.wait_ge(qk_copied, 3 * (t + 1))
                    act.wait_ge(rope_copied, t + 1)
                    if t >= 2:
                        act.wait_ge(qk_ready, t - 1)
                    act.activation(sq[:, t % 2], qk[:, t % 2], ACT.Square).then_inc(squared, 1)

                def columns(t):
                    act.wait_ge(own, 3 + 2 * (t + 1))
                    act.activation(rstd[:, t % 2, :], ssum[:, t % 2, :], ACT.Sqrt).then_inc(rstd_ready, 1)
                    for g in range(0, GROUPS, 2):
                        n = GROUPS * t + g
                        act.wait_ge(turned, n + 1)
                        act.activation(head_columns(n), turn[n % 3][0:QK, :].rearrange("p (h n) -> p h n", h=4),
                                       ACT.Copy).then_inc(out_act, 1)

                for t in range(TILES + 1):
                    if t < TILES:
                        up(t)
                    if t:
                        columns(t - 1)
                    if t == 0:
                        act.wait_ge(angles, 2)
                        act.activation(sin[:, :, :], ang[:, :, :], ACT.Sin).then_inc(trig, 1)
                        act.activation(cos[:, :, :], shifted[:, :, :], ACT.Sin).then_inc(trig, 1)

            @block.vector
            def _(dve):
                mine = Own(dve, own)
                dve.wait_ge(lat_summed, 2 * TILES)
                dve.tensor_scalar(lat_sum[:, 0, :], lat_sum[:, 0, :], 1.0 / Q_LORA, RMS_EPS, ALU.mult, ALU.add).then_inc(own, 1)
                dve.tensor_scalar(lat_sum[:, 1, :], lat_sum[:, 1, :], 1.0 / KV_LORA, RMS_EPS, ALU.mult, ALU.add).then_inc(own, 1)
                mine.n = 2
                dve.wait_ge(own, 2)
                mine.link(dve.reciprocal(lat_sum[:, :, :], lat_sum[:, :, :]))
                dve.wait_ge(here, HERE)

                def up(t):
                    dve.wait_ge(lat_rstd_ready, 1)
                    if t >= 2:
                        dve.wait_ge(lat_turned, t - 1)
                    for part, (lo, hi) in enumerate(((0, Q_LORA), (Q_LORA, Q_LORA + KV_LORA))):
                        dve.scalar_tensor_tensor(out=lat_n[:, t % 2, lo:hi], in0=latents[:, t, lo:hi],
                                                 scalar=lat_rstd[:, part, t:t + 1], in1=lat_gain[:, lo:hi],
                                                 op0=ALU.mult, op1=ALU.mult).then_inc(lat_ready, 1)

                def reduce_angles():
                    ROUND = 1.5 * 2 ** 23
                    TURN = (6.28125, 0.0019350051879882812, 2 * np.pi - 6.28125 - 0.0019350051879882812)
                    seq = Own(dve, ang_own)
                    seq.link(dve.tensor_copy(pos[:, :], pos_i[:, :]))
                    dve.wait_ge(freq_set, HALF)
                    seq.link(dve.tensor_tensor(ang[:, :, :], over(pos[:, :].unsqueeze(2), (P, TILES, HALF)),
                                               over(freq[:, :].unsqueeze(1), (P, TILES, HALF)), ALU.mult))
                    seq.link(dve.tensor_scalar(turns[:, :, :], ang[:, :, :], float(1 / (2 * np.pi)), None, ALU.mult))
                    seq.link(dve.tensor_scalar(turns[:, :, :], turns[:, :, :], ROUND, None, ALU.add))
                    seq.link(dve.tensor_scalar(turns[:, :, :], turns[:, :, :], -ROUND, None, ALU.add))
                    for part in TURN:
                        seq.link(dve.scalar_tensor_tensor(out=ang[:, :, :], in0=turns[:, :, :], scalar=-float(part),
                                                          in1=ang[:, :, :], op0=ALU.mult, op1=ALU.add))
                    pi = float(np.float32(3.1415925))
                    seq.link(dve.tensor_scalar(ang[:, :, :], ang[:, :, :], pi, -pi, ALU.min, ALU.max))
                    seq.link(dve.tensor_scalar(turns[:, :, :], ang[:, :, :], float(np.pi / 2), -2 * float(np.pi), ALU.is_gt, ALU.mult))
                    seq.link(dve.scalar_tensor_tensor(out=shifted[:, :, :], in0=ang[:, :, :], scalar=float(np.pi / 2),
                                                      in1=turns[:, :, :], op0=ALU.add, op1=ALU.add))
                    dve.tensor_scalar(shifted[:, :, :], shifted[:, :, :], pi, -pi, ALU.min, ALU.max).then_inc(angles, 1)
                    dve.engine_nop().then_inc(angles, 1)

                def columns(t):
                    b = t % 2
                    dve.wait_ge(squared, t + 1)
                    if t >= 2:
                        dve.wait_ge(rstd_ready, t - 1)
                    ins = dve.tensor_reduce(ssum[:, b, :], sq[:, b], X_AXIS, ALU.add)
                    ins.then_inc(reduced, 1)
                    dve.wait_ge(reduced, t + 1)
                    mine.link(dve.tensor_scalar(ssum[:, b, :], ssum[:, b, :], 1.0 / QK, RMS_EPS, ALU.mult, ALU.add))
                    mine.link(dve.reciprocal(ssum[:, b, :], ssum[:, b, :]))
                    dve.wait_ge(rstd_ready, t + 1)
                    rows = qk[:, b]
                    scaled.link(dve.tensor_tensor(rows, rows, over(rstd[:, b, :].unsqueeze(2), (P, HEADS2, QK)), ALU.mult))
                    for part in range(2):
                        half = qk[:, b, part * MLA_HEADS:(part + 1) * MLA_HEADS, :]
                        ins = dve.tensor_tensor(half, half, over(qk_gain[:, part:part + 1, :], (P, MLA_HEADS, QK)), ALU.mult)
                        scaled.n += 1
                        ins.then_inc(scaled.sem, 1)
                    dve.wait_ge(scaled.sem, scaled.n)
                    if t == 0:
                        dve.wait_ge(trig, 2)
                    x1, x2 = qk[:, b, :, NOPE:NOPE + HALF], qk[:, b, :, NOPE + HALF:]
                    rot = sq[:, b].rearrange("p h d -> p (h d)")[:, 0:4 * HEADS2 * HALF].rearrange(
                        "p (n h d) -> p n h d", n=4, h=HEADS2)
                    c, s = (over(m[:, t:t + 1, :], (P, HEADS2, HALF)) for m in (cos, sin))
                    for n, (x, m) in enumerate(((x1, c), (x2, s), (x1, s), (x2, c))):
                        dve.tensor_tensor(rot[:, n], x, m, ALU.mult).then_inc(scaled.sem, 1)
                        scaled.n += 1
                    dve.wait_ge(scaled.sem, scaled.n)
                    scaled.link(dve.tensor_tensor(x1, rot[:, 0], rot[:, 1], ALU.subtract))
                    scaled.n += 1
                    dve.tensor_tensor(x2, rot[:, 2], rot[:, 3], ALU.add).then_inc(scaled.sem, 1)
                    dve.wait_ge(scaled.sem, scaled.n)
                    dve.engine_nop().then_inc(qk_ready, 1)
                    for g in range(1, GROUPS, 2):
                        n = GROUPS * t + g
                        dve.wait_ge(turned, n + 1)
                        dve.tensor_copy(head_columns(n), turn[n % 3][0:QK, :].rearrange("p (h n) -> p h n", h=4)
                                        ).then_inc(out_dve, 1)

                ang_own = ph.sem("ang_own")
                scaled = Own(dve, ph.sem("scaled"))
                for t in range(TILES + 1):
                    if t < TILES:
                        up(t)
                    if t == 0:
                        reduce_angles()
                    if t:
                        columns(t - 1)


def attend(nc, name, iterations, units, stages, scale_of, o_cols, ident, first_pair=0):
    START = 1
    U = len(units)
    BUFS = 4
    groups = [[(lo, min(lo + 4, u["blocks"])) for lo in range(0, u["blocks"], 4)] for u in units]
    first = np.cumsum([0] + [len(g) for g in groups]).tolist()
    G = first[-1] + 2
    assert G % 2 == 0 and first[-1] % BUFS == 0 and U % BUFS == 0
    last_of = [max(n for n, u in enumerate(units) if u["head"] == h) for h in range(2)]
    S = len(stages[0])
    with Phase(nc, name) as ph:
        probs = ph.sb("probs", [P, BUFS, SEQ])
        probs_cols = ph.sb("probs_cols", [P, BUFS, BANK])
        out = ph.sb("out", [P, TILES, P])
        top = ph.sb("top", [P, BUFS])
        bias = ph.sb("bias", [P, BUFS])
        total = ph.sb("total", [P, BUFS])
        inv = ph.sb("inv", [P, BUFS])
        weight = ph.sb("weight", [P, BUFS])
        mark = ph.sb("mark", [P, 1])
        s_ps = [ph.ps(f"scores{i}", (P, 2 * BANK)) for i in range(2)]
        t_ps = [ph.ps(f"turn{i}") for i in range(2)]
        o_ps = [ph.ps(f"values{i}") for i in range(2)]
        (staged, scored, masked, bias_ready, exp_done, turned, copied, valued, inv_ready, weighted, out_ready) = (
            ph.sem(n) for n in ("staged", "scored", "masked", "bias", "exp", "turned", "copied", "valued",
                                "inv", "weighted", "out_ready"))

        with nc.Block() as block:
            @block.gpsimd
            def _(pool):
                def stage(i, h):
                    for m, (to, source, reader) in enumerate(stages[h]):
                        if not isinstance(i, int):
                            before = i * 1 - 1
                            if reader == "scores":
                                pool.wait_ge(scored, before * U + (last_of[h] + 1))
                            elif reader == "values":
                                pool.wait_ge(valued, before * first[-1] + first[last_of[h] + 1])
                            else:
                                pool.wait_ge(out_ready, before * U + (last_of[h] + 1))
                        if not isinstance(i, int) or h * S + m:
                            pool.wait_ge(staged, i * (2 * S) + (h * S + m))
                        pool.tensor_copy(to, source(i)).then_inc(staged, 1)

                for h in range(2):
                    stage(0, h)
                with pool.Fori(1, iterations) as i:
                    for h in range(2):
                        stage(i, h)

            @block.tensor
            def _(pe):
                pe.sem_inc(turned, START)
                with pe.Fori(0, iterations) as i:
                    def score(n):
                        u = units[n]
                        if n == 0 or units[n - 1]["head"] != u["head"]:
                            pe.wait_ge(staged, i * (2 * S) + S * (u["head"] + 1))
                        if n >= 2:
                            pe.wait_ge(masked, i * U + (n - 1))
                        w = u["blocks"] * P
                        for lo in range(0, w, BANK):
                            hi = min(lo + BANK, w)
                            last = pe.matmul(s_ps[n % 2][:, lo:hi], u["q"], u["k"](lo, hi), start=True, stop=True)
                        last.then_inc(scored, 1)

                    def turn(n):
                        pe.wait_ge(exp_done, i * U + (n + 1))
                        for g, (lo, hi) in enumerate(groups[n], first[n]):
                            pe.wait_ge(copied, i * G + (max(g - 1, 0) + START))
                            for b in range(lo, hi):
                                last = pe.transpose(t_ps[g % 2][:, (b - lo) * P:(b - lo + 1) * P],
                                                    probs[:, n % BUFS, b * P:(b + 1) * P], ident[:, :])
                            last.then_inc(turned, 1)

                    def value(n):
                        u = units[n]
                        if n >= 2:
                            pe.wait_ge(out_ready, i * U + (n - 1))
                        for g, (lo, hi) in enumerate(groups[n], first[n]):
                            pe.wait_ge(copied, i * G + (g + 1 + START))
                            for b in range(lo, hi):
                                last = pe.matmul(o_ps[n % 2][:, 0:V_DIM], probs_cols[:, g % BUFS, (b - lo) * P:(b - lo + 1) * P],
                                                 u["v"](b), start=(b == 0), stop=(b == u["blocks"] - 1))
                            last.then_inc(valued, 1)

                    score(0)
                    score(1)
                    for n in range(U):
                        turn(n)
                        if n + 2 < U:
                            score(n + 2)
                        value(n)
                    pe.wait_ge(out_ready, i * U + U)
                    for g in range(2):
                        pe.wait_ge(copied, i * G + (G - 3 + g + START))
                        for j in range(4):
                            last = pe.transpose(t_ps[g][:, j * P:(j + 1) * P], out[:, 4 * g + j, :], ident[:, :])
                        last.then_inc(turned, 1)

            @block.scalar
            def _(act):
                act.sem_inc(copied, START)
                with act.Fori(0, iterations) as i:
                    def exps(n):
                        u = units[n]
                        act.wait_ge(bias_ready, i * U + (n + 1))
                        p = probs[:, n % BUFS, 0:u["blocks"] * P]
                        act.activation(p, p, ACT.Exp, bias=bias[:, n % BUFS:n % BUFS + 1], scale=scale_of(u, 1),
                                       accum_out=total[:, n % BUFS:n % BUFS + 1]).then_inc(exp_done, 1)

                    exps(0)
                    exps(1)
                    for n in range(U):
                        for g, (lo, hi) in enumerate(groups[n], first[n]):
                            act.wait_ge(turned, i * G + (g + 1 + START))
                            if g >= BUFS:
                                act.wait_ge(valued, i * first[-1] + (g - BUFS + 1))
                            w = (hi - lo) * P
                            act.activation(probs_cols[:, g % BUFS, 0:w], t_ps[g % 2][:, 0:w], ACT.Copy).then_inc(copied, 1)
                        if n + 2 < U:
                            exps(n + 2)
                    for g in range(2):
                        act.wait_ge(turned, i * G + (G - 1 + g + START))
                        act.activation(o_cols[:, bass.ds((i + first_pair) * SEQ + g * BANK, BANK)], t_ps[g][:, :],
                                       ACT.Copy).then_inc(copied, 1)

            @block.vector
            def _(dve):
                with dve.Fori(0, iterations) as i:
                    def may_mask(n):
                        dve.wait_ge(scored, i * U + (n + 1))
                        if n >= BUFS:
                            dve.wait_ge(turned, i * G + (first[n - BUFS + 1] + START))

                    def mask(n):
                        u = units[n]
                        b = n % BUFS
                        dve.tensor_tensor_reduce(probs[:, b, 0:u["blocks"] * P], s_ps[n % 2][:, 0:u["blocks"] * P],
                                                 u["mask"], 1.0, -3e38, ALU.add, ALU.max,
                                                 top[:, b:b + 1]).then_inc(masked, 1)

                    def biased(n):
                        b = n % BUFS
                        dve.wait_ge(masked, i * U + (n + 1))
                        dve.tensor_scalar(bias[:, b:b + 1], top[:, b:b + 1], scale_of(units[n], -1), None,
                                          ALU.mult).then_inc(bias_ready, 1)

                    def inverse(n):
                        b = n % BUFS
                        dve.wait_ge(exp_done, i * U + (n + 1))
                        dve.reciprocal(inv[:, b:b + 1], total[:, b:b + 1]).then_inc(inv_ready, 1)

                    def write(n):
                        u, b = units[n], n % BUFS
                        dve.wait_ge(inv_ready, i * U + (n + 1))
                        if u["gate"] is not None:
                            dve.tensor_tensor(weight[:, b:b + 1], inv[:, b:b + 1], u["gate"], ALU.mult).then_inc(weighted, 1)
                        to = out[:, u["tile"], u["head"] * V_DIM:(u["head"] + 1) * V_DIM]
                        dve.wait_ge(valued, i * first[-1] + first[n + 1])
                        if n == 0:
                            dve.wait_ge(turned, i * G + START)
                        if u["gate"] is None:
                            dve.tensor_scalar(to, o_ps[n % 2][:, 0:V_DIM], inv[:, b:b + 1], None, ALU.mult).then_inc(out_ready, 1)
                        else:
                            dve.wait_ge(weighted, i * U + (n + 1))
                            add = to if u["add"] is None else u["add"](i)
                            if u["add"] is None:
                                dve.wait_ge(out_ready, i * U + n)
                            dve.scalar_tensor_tensor(out=to, in0=o_ps[n % 2][:, 0:V_DIM], scalar=weight[:, b:b + 1],
                                                     in1=add, op0=ALU.mult, op1=ALU.add).then_inc(out_ready, 1)

                    for n in range(2):
                        may_mask(n)
                        dve.memset(mark[:, :], 0.0)
                        mask(n)
                        biased(n)
                    for n in range(U):
                        if n + 2 < U:
                            may_mask(n + 2)
                        inverse(n)
                        if n + 2 < U:
                            mask(n + 2)
                        if n + 2 < U:
                            biased(n + 2)
                        write(n)


def mla_attention(nc, q_cols, k_cols, v_rows, o_cols, ident, rows_to_clear):
    with Phase(nc, "mla") as ph:
        causal = ph.sb("causal", [P, SEQ])
        q = ph.sb("q", [P, 2, SEQ])
        k = ph.sb("k", [P, 2, SEQ])
        v = ph.sb("v", [P, 2, TILES, V_DIM])
        zeroed, masked, cleared = ph.sem("zeroed"), ph.sem("masked"), ph.sem("cleared")
        halves = rows_to_clear.rearrange("(b p) (h n) -> b h p n", p=P, n=BANK)
        with nc.Block() as block:
            @block.sync
            def _(sp):
                sp.wait_ge(zeroed, 1)
                for b in range(halves.shape[0]):
                    for h in range(D // BANK):
                        sp.dma_start(halves[b, h], causal[:, 0:BANK]).then_inc(cleared, 16)

            @block.gpsimd
            def _(pool):
                pool.memset(causal[:, :], 0.0).then_inc(zeroed, 1)
                pool.wait_ge(zeroed, 1)
                pool.affine_select(out=causal[:, SEQ - P:], in_=causal[:, SEQ - P:], compare_op=ALU.is_ge, fill=-BIG,
                                   base=0, pattern=[[-1, P]], channel_multiplier=1).then_inc(masked, 1)
                pool.wait_ge(masked, 1)
        units = []
        for h in range(2):
            for t in range(TILES):
                units.append(dict(head=h, tile=t, blocks=t + 1, q=q[0:QK, h, t * P:(t + 1) * P],
                                  k=lambda lo, hi, h=h: k[0:QK, h, lo:hi], mask=causal[:, SEQ - (t + 1) * P:],
                                  v=lambda b, h=h: v[:, h, b, :], gate=None, add=None))
        stages = [[
            (q[0:QK, h, :], lambda i, h=h: q_cols[0:QK, bass.ds((i * 2 + h) * SEQ, SEQ)], "scores"),
            (k[0:QK, h, :], lambda i, h=h: k_cols[0:QK, bass.ds((i * 2 + h) * SEQ, SEQ)], "scores"),
            (v[:, h, :, :], lambda i, h=h: v_rows[:, :, bass.ds((i * 2 + h) * V_DIM, V_DIM)], "values"),
        ] for h in range(2)]
        scale = QK ** -0.5
        attend(nc, "mlaatt", MLA_HEADS // 2, units, stages, lambda u, sign: sign * scale, o_cols, ident)
        nc.sync.wait_ge(cleared, 16 * halves.shape[0] * (D // BANK))


GROUPS = 4
PER_GROUP = 8
EXPERTS = GROUPS * PER_GROUP
TOP_K = 2
HIDDEN = 256
LOGITS = GROUPS + EXPERTS
MORE_BLOCKS = 15
BLOCKS = EXPERTS + MORE_BLOCKS
WEIGHT_BUFS = 4
COMBINE_BUFS = 8


def pool_semaphores(nc, layer):
    counts = {"cleared": 1, "scattered": 1, "x": WEIGHT_BUFS, "y": COMBINE_BUFS}
    return {k: [nc.alloc_semaphore(f"pool{layer}_{k}{i}") for i in range(n)] for k, n in counts.items()}


def load_expert(eng, A, layer, e, w, here):
    gate, up, down = (A[n][layer] for n in ("moe_w_gate", "moe_w_up", "moe_w_down"))
    eng.dma_start(w["gate"], gate[bass.ds(e, 1)].rearrange("o (p c) f -> p (o c f)", p=P)).then_inc(here, 16)
    eng.dma_start(w["up"], up[bass.ds(e, 1)].rearrange("o (p c) f -> p (o c f)", p=P)).then_inc(here, 16)
    eng.dma_start(w["down"], down[bass.ds(e, 1)].rearrange("o (p c) n -> p (o c n)", p=P)).then_inc(here, 16)


def route(nc, name, layer, h_cols, ident, ones, slots, gates, index, more, row_token, pool_sems, A):
    with Phase(nc, name) as ph:
        T, G4, E8 = TILES, GROUPS, PER_GROUP
        w = ph.sb("w", [P, CHUNKS, LOGITS])
        bias = ph.sb("bias", [P, LOGITS])
        before = ph.sb("before", [P, P])
        rank_code = ph.sb("rank_code", [P, E8])
        first_slot = ph.sb("first_slot", [P, EXPERTS])
        logits = ph.sb("logits", [P, T, LOGITS])
        group_top = ph.sb("group_top", [P, T])
        group_hot = ph.sb("group_hot", [P, T, G4])
        code = ph.sb("code", [P, T])
        shifted = ph.sb("shifted", [P, T, G4])
        picked = ph.sb("picked", [P, T, G4, E8])
        inner = ph.sb("inner", [P, T, E8])
        inner_top = ph.sb("inner_top", [P, TOP_K, T])
        hot = ph.sb("hot", [P, TOP_K, T, E8])
        group_weight = ph.sb("group_weight", [P, T])
        ratio = ph.sb("ratio", [P, T])
        share = ph.sb("share", [P, T])
        chosen = ph.sb("chosen", [P, TOP_K, T, G4, E8])
        member = ph.sb("member", [P, T, EXPERTS])
        count = ph.sb("count", [P, T + 1, EXPERTS])
        rank = ph.sb("rank", [P, T, EXPERTS])
        extra = ph.sb("extra", [P, EXPERTS])
        extra_end = ph.sb("extra_end", [P, EXPERTS])
        later = ph.sb("later", [P, EXPERTS])
        beyond = ph.sb("beyond", [P, T, EXPERTS])
        slot_f = ph.sb("slot_f", [P, TOP_K, T])
        turn_no = ph.sb("turn_no", [P, MORE_BLOCKS])
        passed = ph.sb("passed", [1, MORE_BLOCKS, EXPERTS])
        more_f = ph.sb("more_f", [1, MORE_BLOCKS + 1])
        token = ph.sb("token", [P, T], I32)
        nobody = ph.sb("nobody", [BLOCKS, P], I32)
        token_rows = ph.sb("token_rows", [BLOCKS, P], I32)
        token_rows_f = ph.sb("token_rows_f", [BLOCKS, P])
        logit_ps = ph.ps("logit_ps")
        rank_ps = ph.ps("rank_ps")
        count_ps = ph.ps("count_ps")
        index_ps = ph.ps("index_ps")
        (here, made, logits_done, own, exps_ready, exped, counted, slots_ready, rows_here,
         rows_f, index_turned) = (ph.sem(n) for n in (
             "here", "made", "logits", "own", "exps_ready", "exped", "counted", "slots", "rows_here", "rows_f",
             "index_turned"))
        cleared, scattered = pool_sems["cleared"][0], pool_sems["scattered"][0]

        with nc.Block() as block:
            @block.sync
            def _(sp):
                with nc.allow_non_contiguous_dma(reason="small weights, once"):
                    sp.dma_start(w[:, :, 0:G4], A["moe_router_group"][layer].rearrange("(p c) n -> p c n", p=P)).then_inc(here, 16)
                    sp.dma_start(w[:, :, G4:], A["moe_router_expert"][layer].rearrange("(p c) n -> p c n", p=P)).then_inc(here, 16)
                sp.dma_start(bias[:, 0:G4], A["moe_router_group_b"][layer].partition_broadcast(P)).then_inc(here, 16)
                sp.dma_start(bias[:, G4:], A["moe_router_expert_b"][layer].partition_broadcast(P)).then_inc(here, 16)
                sp.wait_ge(scattered, 16 * TOP_K * T)
                sp.dma_start(token_rows[:, :], row_token.rearrange("(b r) o -> b (r o)", r=P)).then_inc(rows_here, 16)

            @block.gpsimd
            def _(pool):
                pool.memset(nobody[:, :], 0).then_inc(made, 1)
                pool.memset(before[:, :], 1.0).then_inc(made, 1)
                pool.iota(token[:, :], pattern=[[P, T]], base=0, channel_multiplier=1).then_inc(made, 1)
                pool.iota(first_slot[:, :], pattern=[[P, EXPERTS]], base=0, channel_multiplier=0,
                          allow_small_or_imprecise_dtypes=True).then_inc(made, 1)
                pool.iota(rank_code[:, :], pattern=[[-1, E8]], base=E8, channel_multiplier=0,
                          allow_small_or_imprecise_dtypes=True).then_inc(made, 1)
                pool.iota(turn_no[:, :], pattern=[[1, MORE_BLOCKS]], base=0, channel_multiplier=0,
                          allow_small_or_imprecise_dtypes=True).then_inc(made, 1)
                pool.wait_ge(made, 6)
                pool.affine_select(out=before[:, :], in_=before[:, :], compare_op=ALU.is_gt, fill=0.0, base=0,
                                   pattern=[[1, P]], channel_multiplier=-1).then_inc(made, 1)
                pool.dma_start(row_token.rearrange("(b r) o -> b (r o)", r=P), nobody[:, :]).then_inc(cleared, 16)
                pool.wait_ge(cleared, 16)
                pool.wait_ge(slots_ready, 1)
                for k in range(TOP_K):
                    for t in range(T):
                        pool.indirect_dma_start(out=row_token, out_offset=bass.IndirectOffsetOnAxis(
                            ap=slots[:, k, t:t + 1].bitcast(U32), axis=0), in_=token[:, t:t + 1], in_offset=None
                            ).then_inc(scattered, 16)
                pool.wait_ge(scattered, 16 * TOP_K * T)

            @block.tensor
            def _(pe):
                pe.wait_ge(here, 64)
                for t in range(T):
                    for c in range(CHUNKS):
                        last = pe.matmul(logit_ps[:, t * LOGITS:(t + 1) * LOGITS], h_cols[:, c, t * P:(t + 1) * P],
                                         w[:, c, :], start=(c == 0), stop=(c == CHUNKS - 1))
                last.then_inc(logits_done, 1)
                pe.wait_ge(exps_ready, 3)
                pe.wait_ge(made, 7)
                m = member[:, :, :].rearrange("p t e -> p (t e)")
                pe.matmul(rank_ps[:, 0:T * EXPERTS], before[:, :], m, start=True, stop=True)
                pe.matmul(count_ps[:, 0:T * EXPERTS], ones[:, :], m, start=True, stop=True).then_inc(counted, 1)
                pe.wait_ge(rows_f, 1)
                pe.transpose(index_ps[:, 0:BLOCKS], token_rows_f[:, :], ident[0:BLOCKS, 0:BLOCKS]).then_inc(index_turned, 1)

            @block.scalar
            def _(act):
                act.wait_ge(exps_ready, 1)
                act.activation(shifted[:, :, :], shifted[:, :, :], ACT.Exp).then_inc(exped, 1)
                act.wait_ge(exps_ready, 2)
                act.activation(ratio[:, :], ratio[:, :], ACT.Exp).then_inc(exped, 1)

            @block.vector
            def _(dve):
                mine = Own(dve, own)

                def first_hot(to, values, top, codes, width):
                    mine.link(dve.tensor_reduce(top, values, X_AXIS, ALU.max))
                    mine.link(dve.tensor_tensor(to, values, over(top.unsqueeze(2), (P, T, width)), ALU.is_equal))
                    mine.link(dve.tensor_tensor(to, to, over(codes.unsqueeze(1), (P, T, width)), ALU.mult))
                    mine.link(dve.tensor_reduce(code[:, :], to, X_AXIS, ALU.max))
                    mine.link(dve.tensor_tensor(to, to, over(code[:, :].unsqueeze(2), (P, T, width)), ALU.is_equal))

                dve.wait_ge(here, 64)
                dve.wait_ge(made, 7)
                dve.wait_ge(logits_done, 1)
                mine.link(dve.tensor_tensor(logits[:, :, :], logit_ps[:, 0:T * LOGITS].rearrange("p (t n) -> p t n", t=T),
                                            over(bias[:, :].unsqueeze(1), (P, T, LOGITS)), ALU.add))
                group = logits[:, :, 0:G4]
                first_hot(group_hot[:, :, :], group, group_top[:, :], rank_code[:, E8 - G4:], G4)
                dve.tensor_tensor(shifted[:, :, :], group, over(group_top[:, :].unsqueeze(2), (P, T, G4)),
                                  ALU.subtract).then_inc(exps_ready, 1)
                mine.link(dve.tensor_tensor(picked[:, :, :, :], logits[:, :, G4:].rearrange("p t (g e) -> p t g e", g=G4),
                                            over(group_hot[:, :, :].unsqueeze(3), (P, T, G4, E8)), ALU.mult))
                mine.link(dve.tensor_reduce(inner[:, :, :], picked[:, :, :, :].rearrange("p t g e -> p t e g"),
                                            X_AXIS, ALU.add))
                first_hot(hot[:, 0], inner[:, :, :], inner_top[:, 0, :], rank_code[:, :], E8)
                mine.link(dve.scalar_tensor_tensor(out=inner[:, :, :], in0=hot[:, 0], scalar=-BIG, in1=inner[:, :, :],
                                                   op0=ALU.mult, op1=ALU.add))
                first_hot(hot[:, 1], inner[:, :, :], inner_top[:, 1, :], rank_code[:, :], E8)
                dve.tensor_tensor(ratio[:, :], inner_top[:, 1, :], inner_top[:, 0, :], ALU.subtract).then_inc(exps_ready, 1)
                for k in range(TOP_K):
                    mine.link(dve.tensor_tensor(chosen[:, k], over(group_hot[:, :, :].unsqueeze(3), (P, T, G4, E8)),
                                                over(hot[:, k].unsqueeze(2), (P, T, G4, E8)), ALU.mult))
                dve.tensor_tensor(member[:, :, :], chosen[:, 0].rearrange("p t g e -> p t (g e)"),
                                  chosen[:, 1].rearrange("p t g e -> p t (g e)"), ALU.add).then_inc(exps_ready, 1)
                dve.wait_ge(exped, 2)
                mine.link(dve.tensor_reduce(group_weight[:, :], shifted[:, :, :], X_AXIS, ALU.add))
                mine.link(dve.reciprocal(group_weight[:, :], group_weight[:, :]))
                mine.link(dve.tensor_scalar(share[:, :], ratio[:, :], 1.0, None, ALU.add))
                mine.link(dve.reciprocal(share[:, :], share[:, :]))
                mine.link(dve.tensor_tensor(gates[:, 0, :], share[:, :], group_weight[:, :], ALU.mult))
                mine.link(dve.tensor_tensor(gates[:, 1, :], gates[:, 0, :], ratio[:, :], ALU.mult))
                dve.wait_ge(counted, 1)
                mine.link(dve.memset(count[:, 0, :], 0.0))
                for t in range(T):
                    mine.link(dve.tensor_tensor(count[:, t + 1, :], count_ps[:, t * EXPERTS:(t + 1) * EXPERTS],
                                                count[:, t, :], ALU.add))
                mine.link(dve.tensor_tensor(rank[:, :, :], rank_ps[:, 0:T * EXPERTS].rearrange("p (t e) -> p t e", t=T),
                                            count[:, 0:T, :], ALU.add))
                total = count[:, T, :]
                mine.link(dve.tensor_scalar(extra[:, :], total, float(P), None, ALU.is_gt))
                for j in range(2, SEQ // P):
                    mine.link(dve.scalar_tensor_tensor(out=extra[:, :], in0=total, scalar=float(j * P), in1=extra[:, :],
                                                       op0=ALU.is_gt, op1=ALU.add))
                mine.link(dve.tensor_tensor_scan(extra_end[:, :], ones[:, 0:EXPERTS], extra[:, :], 0.0, ALU.mult, ALU.add))
                mine.link(dve.tensor_tensor(later[:, :], extra_end[:, :], extra[:, :], ALU.subtract))
                mine.link(dve.tensor_scalar(later[:, :], later[:, :], float(P), float((EXPERTS - 1) * P), ALU.mult, ALU.add))
                mine.link(dve.tensor_tensor(later[:, :], later[:, :], first_slot[:, :], ALU.subtract))
                wide = (P, T, EXPERTS)
                mine.link(dve.tensor_scalar(beyond[:, :, :], rank[:, :, :], float(P), None, ALU.is_ge))
                mine.link(dve.tensor_tensor(beyond[:, :, :], beyond[:, :, :], over(later[:, :].unsqueeze(1), wide), ALU.mult))
                mine.link(dve.tensor_tensor(rank[:, :, :], rank[:, :, :], beyond[:, :, :], ALU.add))
                mine.link(dve.tensor_tensor(rank[:, :, :], rank[:, :, :], over(first_slot[:, :].unsqueeze(1), wide), ALU.add))
                for k in range(TOP_K):
                    mine.link(dve.tensor_tensor(beyond[:, :, :], rank[:, :, :],
                                                chosen[:, k].rearrange("p t g e -> p t (g e)"), ALU.mult))
                    mine.link(dve.tensor_reduce(slot_f[:, k, :], beyond[:, :, :], X_AXIS, ALU.add))
                dve.tensor_copy(slots[:, :, :], slot_f[:, :, :]).then_inc(slots_ready, 1)
                mine.link(dve.tensor_tensor(passed[:, :, :], over(extra_end[0:1, :].unsqueeze(1), (1, MORE_BLOCKS, EXPERTS)),
                                            over(turn_no[0:1, :].unsqueeze(2), (1, MORE_BLOCKS, EXPERTS)), ALU.is_le))
                mine.link(dve.tensor_reduce(more_f[:, 0:MORE_BLOCKS], passed[:, :, :], X_AXIS, ALU.add))
                mine.link(dve.tensor_scalar(more_f[:, 0:MORE_BLOCKS], more_f[:, 0:MORE_BLOCKS], float(EXPERTS - 1), None, ALU.min))
                mine.link(dve.tensor_copy(more_f[:, MORE_BLOCKS:], extra_end[0:1, EXPERTS - 1:]))
                dve.tensor_copy(more[:, :], more_f[:, :])
                dve.wait_ge(rows_here, 16)
                dve.tensor_copy(token_rows_f[:, :], token_rows[:, :]).then_inc(rows_f, 1)
                dve.wait_ge(index_turned, 1)
                dve.tensor_copy(index[:, :], index_ps[:, 0:BLOCKS])


def experts(nc, name, layer, w, w_here, ident, index, more, h_dram, y_dram, pool_sems, A):
    LEAD = 4
    B = WEIGHT_BUFS
    with Phase(nc, name) as ph:
        column = ph.sb("column", [P, B], I32)
        x_rows = ph.sb("x", [P, B, D])
        x_cols = ph.sb("x_cols", [P, 2, CHUNKS, P])
        sig = ph.sb("sig", [P, 2, HIDDEN])
        hid = ph.sb("hid", [P, 2, HIDDEN])
        hid_cols = ph.sb("hid_cols", [P, 2, 2, P])
        y = ph.sb("y", [P, 2, D])
        mark = ph.sb("mark", [P, 1])
        beat = ph.sb("beat", [P, 1])
        set_up = ph.sem("set_up")
        x_ps = [ph.ps(f"x_ps{i}") for i in range(2)]
        gu_ps = [ph.ps(f"gu_ps{i}") for i in range(2)]
        hid_ps = ph.ps("hid_ps")
        y_ps = [ph.ps(f"y_ps{i}") for i in range(2)]
        column_ready, x_here = ph.sem("column"), pool_sems["x"]
        (x_turned, x_act, x_dve, gu_done, sig_ready, silu_ready, hid_ready, hid_turned, hid_copied, down_done,
         y_act, y_dve) = (ph.sem(n) for n in (
             "x_turned", "x_act", "x_dve", "gu", "sig", "silu", "hid", "hid_turned", "hid_copied", "down",
             "y_act", "y_dve"))
        stored = [ph.sem(f"stored{i}") for i in range(2)]
        USES = EXPERTS // 2

        def count_up(eng, sems):
            for s in sems:
                eng.sem_inc(s, LEAD)

        def extras(eng, body):
            used = eng.value_load(more[0:1, MORE_BLOCKS:], min_val=0, max_val=MORE_BLOCKS)
            with eng.Fori(0, MORE_BLOCKS) as j:
                with eng.If(j < used):
                    body(j)
            return used

        with nc.Block() as block:
            @block.sync
            def _(sp):
                with sp.Fori(1, EXPERTS // B) as i:
                    for s in range(B):
                        n = i * B + s
                        sp.wait_ge(down_done, n + (LEAD - B + 1))
                        load_expert(sp, A, layer, n, w[s], w_here[s])

                def extra(j):
                    sp.wait_ge(down_done, j + (EXPERTS + LEAD))
                    e = sp.value_load(more[0:1, bass.ds(j, 1)], min_val=0, max_val=EXPERTS - 1)
                    load_expert(sp, A, layer, e, w[0], w_here[0])

                extras(sp, extra)

            @block.gpsimd
            def _(pool):
                def gather(n, s):
                    pool.wait_ge(x_turned, n + (LEAD - B + 1))
                    pool.tensor_copy(column[:, s:s + 1], index[:, bass.ds(n, 1)]).then_inc(column_ready, 1)
                    pool.wait_ge(column_ready, n + 1)
                    pool.tensor_tensor(beat[:, :], beat[:, :], beat[:, :], ALU.add)
                    pool.indirect_dma_start(out=x_rows[:, s, :], out_offset=None, in_=h_dram,
                                            in_offset=bass.IndirectOffsetOnAxis(ap=column[:, s:s + 1].bitcast(U32), axis=0)
                                            ).then_inc(x_here[s], 16)

                pool.memset(beat[:, :], 0.0).then_inc(set_up, 1)
                pool.memset(mark[:, :], 0.0).then_inc(set_up, 1)
                pool.wait_ge(set_up, 2)
                with pool.Fori(0, EXPERTS // B) as i:
                    for s in range(B):
                        gather(i * B + s, s)

                def extra(j):
                    pool.wait_ge(x_turned, j + (EXPERTS + LEAD))
                    gather(j + EXPERTS, 0)

                extras(pool, extra)

            @block.tensor
            def _(pe):
                count_up(pe, (x_turned, gu_done, hid_turned, down_done))

                def turn_x(n, s, use):
                    pe.wait_ge(x_here[s], use * 16)
                    pe.wait_ge(x_act, n + LEAD)
                    pe.wait_ge(x_dve, n + LEAD)
                    spread = x_rows[:, s, :].rearrange("n (p c) -> n c p", c=CHUNKS)
                    for c in range(CHUNKS):
                        last = pe.transpose(x_ps[c // 4][:, c % 4 * P:(c % 4 + 1) * P], spread[:, c, :], ident[:, :])
                    last.then_inc(x_turned, 1)

                def gate_up(n, s, use):
                    pe.wait_ge(w_here[s], use * 48)
                    pe.wait_ge(x_act, n + (LEAD + 1))
                    pe.wait_ge(x_dve, n + (LEAD + 1))
                    pe.wait_ge(hid_ready, n + (LEAD - 1))
                    for k, m in enumerate(("gate", "up")):
                        wm = w[s][m].rearrange("p (c f) -> p c f", c=CHUNKS)
                        for c in range(CHUNKS):
                            last = pe.matmul(gu_ps[s % 2][:, k * HIDDEN:(k + 1) * HIDDEN], x_cols[:, s % 2, c, :],
                                             wm[:, c, :], start=(c == 0), stop=(c == CHUNKS - 1))
                    last.then_inc(gu_done, 1)

                def turn_hidden(n, s):
                    pe.wait_ge(hid_ready, n + (LEAD + 1))
                    pe.wait_ge(hid_copied, n + LEAD)
                    spread = hid[:, s % 2, :].rearrange("n (p c) -> n c p", c=2)
                    for c in range(2):
                        last = pe.transpose(hid_ps[:, c * P:(c + 1) * P], spread[:, c, :], ident[:, :])
                    last.then_inc(hid_turned, 1)

                def down(n, s):
                    pe.wait_ge(hid_copied, n + (LEAD + 1))
                    pe.wait_ge(y_act, n + LEAD)
                    pe.wait_ge(y_dve, n + LEAD)
                    wm = w[s]["down"].rearrange("p (c n) -> p c n", c=2)
                    for half in range(2):
                        for c in range(2):
                            last = pe.matmul(y_ps[half][:, :], hid_cols[:, s % 2, c, :],
                                             wm[:, c, half * BANK:(half + 1) * BANK], start=(c == 0), stop=(c == 1))
                    last.then_inc(down_done, 1)

                with pe.Fori(0, EXPERTS // B) as i:
                    turn_x(i * B, 0, i + 1)
                    for s in range(B):
                        n = i * B + s
                        gate_up(n, s, i + 1)
                        if s + 1 < B:
                            turn_x(n + 1, s + 1, i + 1)
                        turn_hidden(n, s)
                        down(n, s)

                def extra(j):
                    n = j + EXPERTS
                    use = j + (EXPERTS // B + 1)
                    turn_x(n, 0, use)
                    gate_up(n, 0, use)
                    turn_hidden(n, 0)
                    down(n, 0)

                extras(pe, extra)

            def copy_x(eng, op, n, s, half, sem):
                eng.wait_ge(x_turned, n + (LEAD + 1))
                eng.wait_ge(gu_done, n + (LEAD - 1))
                op(x_cols[:, s % 2, 4 * half:4 * half + 4, :].rearrange("p c n -> p (c n)"), x_ps[half][:, :]).then_inc(sem, 1)

            @block.scalar
            def _(act):
                count_up(act, (x_act, sig_ready, hid_copied, y_act))
                for b in range(2):
                    act.sem_inc(stored[b], 16)

                def copy(to, source):
                    return act.activation(to, source, ACT.Copy)

                def sigmoid(n, s):
                    act.wait_ge(gu_done, n + (LEAD + 1))
                    act.wait_ge(hid_ready, n + (LEAD - 1))
                    act.activation(sig[:, s % 2, :], gu_ps[s % 2][:, 0:HIDDEN], ACT.Sigmoid).then_inc(sig_ready, 1)

                def copy_hidden(n, s):
                    act.wait_ge(hid_turned, n + (LEAD + 1))
                    act.wait_ge(down_done, n + (LEAD - 1))
                    copy(hid_cols[:, s % 2, :, :].rearrange("p c n -> p (c n)"), hid_ps[:, 0:HIDDEN]).then_inc(hid_copied, 1)

                def send_y(n, s, uses):
                    act.wait_ge(down_done, n + (LEAD + 1))
                    act.wait_ge(stored[s % 2], uses * 16 + 16)
                    copy(y[:, s % 2, 0:BANK], y_ps[0][:, :]).then_inc(y_act, 1)
                    act.wait_ge(y_act, n + (LEAD + 1))
                    act.wait_ge(y_dve, n + (LEAD + 1))
                    act.dma_start(y_dram[bass.ds(n * P, P), :], y[:, s % 2, :]).then_inc(stored[s % 2], 16)

                with act.Fori(0, EXPERTS // B) as i:
                    copy_x(act, copy, i * B, 0, 0, x_act)
                    for s in range(B):
                        n = i * B + s
                        sigmoid(n, s)
                        if s + 1 < B:
                            copy_x(act, copy, n + 1, s + 1, 0, x_act)
                        copy_hidden(n, s)
                        send_y(n, s, i * (B // 2) + s // 2)
                act.wait_ge(stored[1], 16 * USES + 16)

                def extra(j):
                    n = j + EXPERTS
                    copy_x(act, copy, n, 0, 0, x_act)
                    sigmoid(n, 0)
                    copy_hidden(n, 0)
                    send_y(n, 0, j + USES)

                used = extras(act, extra)
                act.wait_ge(set_up, 2)
                act.wait_ge(stored[0], used * 16 + (16 * USES + 16))
                act.activation(mark[:, :], mark[:, :], ACT.Copy)

            @block.vector
            def _(dve):
                count_up(dve, (x_dve, silu_ready, hid_ready, y_dve))

                def hidden(n, s):
                    dve.wait_ge(sig_ready, n + (LEAD + 1))
                    b = s % 2
                    dve.tensor_tensor(sig[:, b, :], gu_ps[b][:, 0:HIDDEN], sig[:, b, :], ALU.mult).then_inc(silu_ready, 1)
                    dve.wait_ge(silu_ready, n + (LEAD + 1))
                    dve.wait_ge(hid_turned, n + (LEAD - 1))
                    dve.tensor_tensor(hid[:, b, :], gu_ps[b][:, HIDDEN:], sig[:, b, :], ALU.mult).then_inc(hid_ready, 1)

                def copy_y(n, s, uses):
                    dve.wait_ge(down_done, n + (LEAD + 1))
                    dve.wait_ge(stored[s % 2], uses * 16 + 16)
                    dve.tensor_copy(y[:, s % 2, BANK:], y_ps[1][:, :]).then_inc(y_dve, 1)

                with dve.Fori(0, EXPERTS // B) as i:
                    copy_x(dve, dve.tensor_copy, i * B, 0, 1, x_dve)
                    for s in range(B):
                        n = i * B + s
                        hidden(n, s)
                        if s + 1 < B:
                            copy_x(dve, dve.tensor_copy, n + 1, s + 1, 1, x_dve)
                        copy_y(n, s, i * (B // 2) + s // 2)

                def extra(j):
                    n = j + EXPERTS
                    copy_x(dve, dve.tensor_copy, n, 0, 1, x_dve)
                    hidden(n, 0)
                    copy_y(n, 0, j + USES)

                extras(dve, extra)


def combine(nc, name, x_rows, slots, gates, y_dram, pool_sems):
    BUFS = COMBINE_BUFS
    with Phase(nc, name) as ph:
        rows = ph.sb("rows", [P, BUFS, D])
        here = pool_sems["y"]
        added = ph.sem("added")
        with nc.Block() as block:
            @block.gpsimd
            def _(pool):
                for n in range(TOP_K * TILES):
                    t, k = n // TOP_K, n % TOP_K
                    if n >= BUFS:
                        pool.wait_ge(added, n - BUFS + 1)
                    pool.indirect_dma_start(out=rows[:, n % BUFS, :], out_offset=None, in_=y_dram,
                                            in_offset=bass.IndirectOffsetOnAxis(ap=slots[:, k, t:t + 1].bitcast(U32), axis=0)
                                            ).then_inc(here[n % BUFS], 16)

            @block.vector
            def _(dve):
                for n in range(TOP_K * TILES):
                    t, k = n // TOP_K, n % TOP_K
                    dve.wait_ge(here[n % BUFS], 16 * (n // BUFS + 1))
                    if k:
                        dve.wait_ge(added, n)
                    dve.scalar_tensor_tensor(out=x_rows[:, t, :], in0=rows[:, n % BUFS, :], scalar=gates[:, k, t:t + 1],
                                             in1=x_rows[:, t, :], op0=ALU.mult, op1=ALU.add).then_inc(added, 1)


def moe(nc, layer, x_rows, ident, ones, scratch, pool_sems, A):
    h_dram, y_dram, row_token = scratch
    with Phase(nc, f"moe{layer}") as ph:
        slots = ph.sb("slots", [P, TOP_K, TILES], I32)
        gates = ph.sb("gates", [P, TOP_K, TILES])
        index = ph.sb("index", [P, BLOCKS], I32)
        more = ph.sb("more", [1, MORE_BLOCKS + 1], I32)
        with Phase(nc, f"moew{layer}") as wp:
            w, w_here = [], []
            for s in range(WEIGHT_BUFS):
                w.append({"gate": wp.sb(f"gate{s}", [P, CHUNKS * HIDDEN])[:, :], "up": wp.sb(f"up{s}", [P, CHUNKS * HIDDEN])[:, :],
                          "down": wp.sb(f"down{s}", [P, 2 * D])[:, :]})
                w_here.append(wp.sem(f"here{s}"))
                load_expert(nc.sync, A, layer, s, w[s], w_here[s])
            with Phase(nc, f"moeh{layer}") as hp:
                h_cols = hp.sb("h_cols", [P, CHUNKS, SEQ])
                norm_columns(nc, f"normf{layer}", x_rows, A["norm_ffn"][layer], ident, h_cols, h_dram)
                route(nc, f"route{layer}", layer, h_cols, ident, ones, slots, gates, index, more, row_token,
                      pool_sems, A)
            experts(nc, f"experts{layer}", layer, w, w_here, ident, index, more, h_dram, y_dram, pool_sems, A)
        combine(nc, f"combine{layer}", x_rows, slots, gates, y_dram, pool_sems)


NSA_HEADS = 16
PAIRS = NSA_HEADS // 2
KV_GROUPS = 2
GROUP_HEADS = NSA_HEADS // KV_GROUPS
HD = 64
Q_WIDTH = NSA_HEADS * HD
KV_WIDTH = KV_GROUPS * HD
BRANCHES = 3
NSA_IN = Q_WIDTH + 6 * KV_WIDTH + BRANCHES * NSA_HEADS
CMP_BLOCK = 32
CMP_STRIDE = 16
CMP_HIDDEN = 128
N_CMP = (SEQ - CMP_BLOCK) // CMP_STRIDE + 1
SLC_BLOCK = 64
N_SLC = SEQ // SLC_BLOCK
WINDOW = 256
WIN_BLOCKS = WINDOW // P + 1
FORCE_SCORE = 1e4
SLOPES = [float(np.float32(2.0 ** (-8.0 * (h + 1) / NSA_HEADS))) for h in range(NSA_HEADS)]
CAUSAL_WIDTH = sum(t + 1 for t in range(TILES)) * P


def causal_at(t):
    return t * (t + 1) // 2 * P


class Turn(Own):

    def __init__(self, eng, sem, i, per_turn):
        super().__init__(eng, sem)
        self.i, self.per_turn = i, per_turn

    def link(self, ins):
        self.n += 1
        ins.then_inc(self.sem, 1)
        self.eng.wait_ge(self.sem, self.i * self.per_turn + self.n)


def nsa_inputs(nc, h_cols, w_in, w_in_here, q_cols, k_cols, v_rows, cmp_cols, gates, ident, A):
    HEADS = NSA_HEADS + 2 * KV_GROUPS
    N = TILES
    KC = Q_WIDTH
    KS = Q_WIDTH + 2 * KV_WIDTH
    GATES = NSA_IN - BRANCHES * NSA_HEADS
    GR = 3
    with Phase(nc, "nsain") as ph:
        gain = ph.sb("gain", [P, HEADS, HD])
        rows = ph.sb("rows", [P, 2, HEADS, HD])
        square = ph.sb("square", [P, HEADS, HD])
        twice = ph.sb("twice", [P, 2, 2 * KV_GROUPS, 2, HD])
        total = ph.sb("total", [P, HEADS])
        rstd = ph.sb("rstd", [P, 2, HEADS])
        q_ps = ph.ps("q_ps", (P, 2 * BANK))
        kv_ps = [ph.ps(f"kv_ps{i}") for i in range(2)]
        gate_ps = ph.ps("gate_ps")
        turn = [ph.ps(f"turn{i}") for i in range(3)]
        (here, gain_ready, cmp_done, cmp_copied, projected, copied, squared, reduced, own, rstd_ready, scaled,
         rows_ready, turned, out_act, out_dve) = (ph.sem(n) for n in (
             "here", "gain", "cmp", "cmp_copied", "projected", "copied", "squared", "reduced", "own", "rstd",
             "scaled", "rows_ready", "turned", "out_act", "out_dve"))

        with nc.Block() as block:
            @block.sync
            def _(sp):
                for h in range(NSA_HEADS):
                    sp.dma_start(gain[:, h, :], A["nsa_q_norm"][0].partition_broadcast(P)).then_inc(here, 16)
                for g in range(KV_GROUPS):
                    sp.dma_start(gain[:, NSA_HEADS + g, :], A["nsa_k_norm_slc"][0].partition_broadcast(P)).then_inc(here, 16)
                    sp.dma_start(gain[:, NSA_HEADS + KV_GROUPS + g, :],
                                 A["nsa_k_norm_win"][0].partition_broadcast(P)).then_inc(here, 16)

            @block.tensor
            def _(pe):
                pe.wait_ge(w_in_here, 16)
                for u in range(4):
                    kind, half = u // 2, u % 2
                    if u >= 2:
                        pe.wait_ge(cmp_copied, u - 1)
                    for c in range(CHUNKS):
                        last = pe.matmul(kv_ps[u % 2][:, :], w_in[:, c, KC + kind * P:KC + (kind + 1) * P],
                                         h_cols[:, c, half * BANK:(half + 1) * BANK], start=(c == 0), stop=(c == CHUNKS - 1))
                    last.then_inc(cmp_done, 1)

                def project(t):
                    if t:
                        pe.wait_ge(copied, 4 * t)
                    else:
                        pe.wait_ge(cmp_copied, 4)
                    for to, lo, hi in ((q_ps[:, 0:BANK], 0, BANK), (q_ps[:, BANK:], BANK, Q_WIDTH),
                                       (kv_ps[0][:, :], KS, GATES), (gate_ps[:, 0:NSA_IN - GATES], GATES, NSA_IN)):
                        for c in range(CHUNKS):
                            last = pe.matmul(to, h_cols[:, c, t * P:(t + 1) * P], w_in[:, c, lo:hi],
                                             start=(c == 0), stop=(c == CHUNKS - 1))
                    last.then_inc(projected, 1)

                def columns(t):
                    pe.wait_ge(rows_ready, 3 * (t + 1))
                    for g in range(GR):
                        n = GR * t + g
                        if n >= 3:
                            pe.wait_ge(out_dve if g == 1 else out_act, t if g == 1 else 2 * (t - 1) + (1 if g == 0 else 2))
                        for j in range(4):
                            b = 4 * g + j
                            source = (rows[:, t % 2, 2 * b:2 * b + 2, :].rearrange("p h d -> p (h d)") if b < PAIRS
                                      else twice[:, t % 2, b - PAIRS, :, :].rearrange("p h d -> p (h d)"))
                            last = pe.transpose(turn[g][:, j * P:(j + 1) * P], source, ident[:, :])
                        last.then_inc(turned, 1)

                for t in range(N + 1):
                    if t < N:
                        project(t)
                    if t:
                        columns(t - 1)

            def column_place(t, g):
                to, b = (q_cols, 4 * g) if g < 2 else (k_cols, 0)
                return to[:, b:b + 4, t * P:(t + 1) * P]

            @block.scalar
            def _(act):
                for u in range(4):
                    act.wait_ge(cmp_done, u + 1)
                    act.activation(cmp_cols[:, u // 2, u % 2 * BANK:(u % 2 + 1) * BANK], kv_ps[u % 2][:, :],
                                   ACT.Copy).then_inc(cmp_copied, 1)

                def take(t):
                    b = t % 2
                    act.wait_ge(projected, t + 1)
                    if t >= 2:
                        act.wait_ge(turned, GR * (t - 1))
                    act.activation(rows[:, b, 0:NSA_HEADS, :].rearrange("p h d -> p (h d)"), q_ps[:, :], ACT.Copy).then_inc(copied, 1)
                    kv = kv_ps[0][:, :].rearrange("p (r two n) -> p r two n", r=2, two=2)
                    act.activation(rows[:, b, NSA_HEADS:, :].rearrange("p (r h) d -> p r (h d)", r=2), kv[:, :, 0, :],
                                   ACT.Copy).then_inc(copied, 1)
                    act.activation(v_rows[:, t, :, :], kv[:, :, 1, :], ACT.Copy).then_inc(copied, 1)
                    act.activation(gates[:, :, :, t].rearrange("p h r -> p r h"),
                                   gate_ps[:, 0:NSA_IN - GATES].rearrange("p (r h) -> p r h", r=BRANCHES),
                                   ACT.Copy).then_inc(copied, 1)
                    act.wait_ge(copied, 4 * t + 4)
                    if t:
                        act.wait_ge(reduced, t)
                    act.activation(square[:, :, :], rows[:, b], ACT.Square).then_inc(squared, 1)

                def columns(t):
                    act.wait_ge(own, 2 * (t + 1))
                    if t >= 2:
                        act.wait_ge(scaled, t - 1)
                    act.activation(rstd[:, t % 2, :], total[:, :], ACT.Sqrt).then_inc(rstd_ready, 1)
                    for g in (0, 2):
                        act.wait_ge(turned, GR * t + g + 1)
                        act.activation(column_place(t, g), turn[g][:, :].rearrange("p (h n) -> p h n", h=4),
                                       ACT.Copy).then_inc(out_act, 1)

                for t in range(N + 1):
                    if t < N:
                        take(t)
                    if t:
                        columns(t - 1)
                act.wait_ge(copied, 4 * N)
                flat = gates[:, :, :, :].rearrange("p h r t -> p (h r t)")
                act.activation(flat, flat, ACT.Sigmoid)

            @block.vector
            def _(dve):
                mine = Own(dve, own)
                dve.wait_ge(here, 16 * HEADS)
                for h in range(NSA_HEADS):
                    dve.tensor_scalar(gain[:, h, :], gain[:, h, :], HD ** -0.5 / SLOPES[h], None, ALU.mult).then_inc(gain_ready, 1)

                def columns(t):
                    b = t % 2
                    dve.wait_ge(squared, t + 1)
                    if t:
                        dve.wait_ge(rstd_ready, t)
                    dve.tensor_reduce(total[:, :], square[:, :, :], X_AXIS, ALU.add).then_inc(reduced, 1)
                    dve.wait_ge(reduced, t + 1)
                    mine.link(dve.tensor_scalar(total[:, :], total[:, :], 1.0 / HD, RMS_EPS, ALU.mult, ALU.add))
                    mine.link(dve.reciprocal(total[:, :], total[:, :]))
                    dve.wait_ge(rstd_ready, t + 1)
                    dve.tensor_tensor(rows[:, b], rows[:, b], over(rstd[:, b, :].unsqueeze(2), (P, HEADS, HD)),
                                      ALU.mult).then_inc(scaled, 1)
                    dve.wait_ge(scaled, t + 1)
                    dve.wait_ge(gain_ready, NSA_HEADS)
                    dve.tensor_tensor(rows[:, b, 0:NSA_HEADS], rows[:, b, 0:NSA_HEADS], gain[:, 0:NSA_HEADS],
                                      ALU.mult).then_inc(rows_ready, 1)
                    for copy in range(2):
                        dve.tensor_tensor(twice[:, b, :, copy, :], rows[:, b, NSA_HEADS:], gain[:, NSA_HEADS:],
                                          ALU.mult).then_inc(rows_ready, 1)
                    dve.wait_ge(turned, GR * t + 2)
                    dve.tensor_copy(column_place(t, 1), turn[1][:, :].rearrange("p (h n) -> p h n", h=4)).then_inc(out_dve, 1)

                for t in range(N):
                    columns(t)


def compress(nc, cmp_cols, k_cmp_cols, v_cmp_rows, ident, A):
    KINDS = ("k", "v")
    with Phase(nc, "cmp") as ph:
        w1 = ph.sb("w1", [P, 2, CMP_BLOCK, CMP_HIDDEN])
        w2 = ph.sb("w2", [P, 2, HD])
        pe_cols = ph.sb("pe_cols", [P, 2, CMP_BLOCK])
        gain = ph.sb("gain", [N_CMP, HD])
        bias = ph.sb("bias", [P, 2])
        pre = ph.sb("pre", [P, 2, KV_GROUPS, N_CMP])
        cube = ph.sb("cube", [P, 2, KV_GROUPS, N_CMP])
        k_rows = ph.sb("k_rows", [N_CMP, KV_GROUPS, HD])
        square = ph.sb("square", [N_CMP, KV_GROUPS, HD])
        total = ph.sb("total", [N_CMP, KV_GROUPS])
        rstd = ph.sb("rstd", [N_CMP, KV_GROUPS])
        twice = ph.sb("twice", [N_CMP, KV_GROUPS, 2, HD])
        hidden = [[ph.ps(f"hidden{k}{g}") for g in range(KV_GROUPS)] for k in range(2)]
        bias_ps = ph.ps("bias_ps")
        out_ps = ph.ps("out_ps")
        v_ps = ph.ps("v_ps")
        turn = ph.ps("turn")
        (here, bias_done, hidden_done, own, cubic_ready, sig_ready, gelu_ready, out_done, mean_ready, rstd_ready,
         keys_ready, turned) = (ph.sem(n) for n in (
             "here", "bias", "hidden", "own", "cubic", "sig", "gelu", "out", "mean", "rstd", "keys", "turned"))

        with nc.Block() as block:
            @block.sync
            def _(sp):
                for k, kind in enumerate(KINDS):
                    for half in range(2):
                        rows = slice(half * HD, (half + 1) * HD)
                        sp.dma_start(w1[rows, k], A[f"nsa_cmp_w1_{kind}"][0].rearrange("(l d) n -> d l n", d=HD)).then_inc(here, 16)
                    sp.dma_start(w2[:, k, :], A[f"nsa_cmp_w2_{kind}"][0]).then_inc(here, 16)
                    with nc.allow_non_contiguous_dma(reason="small, once"):
                        sp.dma_start(pe_cols[0:HD, k, :], A[f"nsa_cmp_pe_{kind}"][0].rearrange("l d -> d l")).then_inc(here, 16)
                sp.dma_start(gain[:, :], A["nsa_k_norm_cmp"][0].partition_broadcast(N_CMP)).then_inc(here, 16)

            @block.tensor
            def _(pe):
                pe.wait_ge(here, 16 * 9)
                for k in range(2):
                    for l in range(CMP_BLOCK):
                        last = pe.matmul(bias_ps[:, k:k + 1], w1[0:HD, k, l, :], pe_cols[0:HD, k, l:l + 1],
                                         start=(l == 0), stop=(l == CMP_BLOCK - 1))
                last.then_inc(bias_done, 1)
                for k in range(2):
                    for l in range(CMP_BLOCK):
                        for g in range(KV_GROUPS):
                            rows = slice(g * HD, (g + 1) * HD)
                            last = pe.matmul(hidden[k][g][:, 0:N_CMP], w1[rows, k, l, :],
                                             cmp_cols[rows, k, l:l + CMP_STRIDE * (N_CMP - 1) + 1:CMP_STRIDE],
                                             start=(l == 0), stop=(l == CMP_BLOCK - 1))
                    last.then_inc(hidden_done, 1)
                pe.wait_ge(gelu_ready, 1)
                for g in range(KV_GROUPS):
                    last = pe.matmul(out_ps[0:N_CMP, g * HD:(g + 1) * HD], pre[:, 0, g, :], w2[:, 0, :], start=True, stop=True)
                last.then_inc(out_done, 1)
                pe.wait_ge(gelu_ready, 2)
                for g in range(KV_GROUPS):
                    for half in range(2):
                        last = pe.matmul(v_ps[half * HD:half * HD + N_CMP, g * HD:(g + 1) * HD], pre[:, 1, g, :],
                                         w2[:, 1, :], start=True, stop=True)
                last.then_inc(out_done, 1)
                pe.wait_ge(keys_ready, 2)
                for g in range(KV_GROUPS):
                    last = pe.transpose(turn[:, g * HD:g * HD + N_CMP], twice[:, g].rearrange("p h d -> p (h d)"),
                                        ident[0:N_CMP, 0:N_CMP])
                last.then_inc(turned, 1)

            @block.scalar
            def _(act):
                for k in range(2):
                    act.wait_ge(cubic_ready, k + 1)
                    act.activation(cube[:, k], cube[:, k], ACT.Sigmoid, scale=float(2 * np.sqrt(2 / np.pi))).then_inc(sig_ready, 1)
                act.wait_ge(mean_ready, 1)
                act.activation(rstd[:, :], total[:, :], ACT.Sqrt).then_inc(rstd_ready, 1)

            @block.vector
            def _(dve):
                mine = Own(dve, own)
                dve.wait_ge(bias_done, 1)
                mine.link(dve.tensor_copy(bias[:, :], bias_ps[:, 0:2]))
                for k in range(2):
                    dve.wait_ge(hidden_done, k + 1)
                    u, c = pre[:, k], cube[:, k]
                    for g in range(KV_GROUPS):
                        mine.link(dve.tensor_scalar(pre[:, k, g, :], hidden[k][g][:, 0:N_CMP], bias[:, k:k + 1], None, ALU.add))
                    mine.link(dve.tensor_tensor(c, u, u, ALU.mult))
                    mine.link(dve.tensor_scalar(c, c, 0.044715, 1.0, ALU.mult, ALU.add))
                    dve.tensor_tensor(c, c, u, ALU.mult).then_inc(cubic_ready, 1)
                    dve.wait_ge(sig_ready, k + 1)
                    dve.tensor_tensor(u, u, c, ALU.mult).then_inc(gelu_ready, 1)
                dve.wait_ge(out_done, 2)
                one = KV_GROUPS * HD
                mine.link(dve.tensor_copy(k_rows[:, :, :].rearrange("p g d -> p (g d)"), out_ps[0:N_CMP, 0:one]))
                for half in range(2):
                    rows = slice(half * HD, half * HD + N_CMP)
                    dve.tensor_copy(v_cmp_rows[rows, :, :].rearrange("p g d -> p (g d)"), v_ps[rows, 0:one])
                mine.link(dve.tensor_tensor(square[:, :, :], k_rows[:, :, :], k_rows[:, :, :], ALU.mult))
                mine.link(dve.tensor_reduce(total[:, :], square[:, :, :], X_AXIS, ALU.add))
                mine.link(dve.tensor_scalar(total[:, :], total[:, :], 1.0 / HD, RMS_EPS, ALU.mult, ALU.add))
                dve.reciprocal(total[:, :], total[:, :]).then_inc(mean_ready, 1)
                dve.wait_ge(rstd_ready, 1)
                shape = (N_CMP, KV_GROUPS, HD)
                mine.link(dve.tensor_tensor(k_rows[:, :, :], k_rows[:, :, :], over(rstd[:, :].unsqueeze(2), shape), ALU.mult))
                for copy in range(2):
                    dve.tensor_tensor(twice[:, :, copy, :], k_rows[:, :, :], over(gain[:, :].unsqueeze(1), shape),
                                      ALU.mult).then_inc(keys_ready, 1)
                dve.wait_ge(turned, 1)
                dve.tensor_copy(k_cmp_cols[:, :, 0:N_CMP], turn[:, 0:KV_GROUPS * HD].rearrange("p (g n) -> p g n", g=KV_GROUPS)[:, :, 0:N_CMP])


def nsa_masks(nc, near, window, near_cmp, seen_cmp, fixed, free, slopes, A):
    ends = slice(CMP_BLOCK - 1, SEQ, CMP_STRIDE)
    with Phase(nc, "masks") as ph:
        key_i = ph.sb("key_i", [P, SEQ], I32)
        key = ph.sb("key", [P, SEQ])
        query_i = ph.sb("query_i", [P, TILES], I32)
        query = ph.sb("query", [P, TILES])
        here, floats, dist, own = (ph.sem(n) for n in ("here", "floats", "dist", "own"))
        with nc.Block() as block:
            @block.sync
            def _(sp):
                sp.dma_start(key_i[:, :], A["positions"][0].partition_broadcast(P)).then_inc(here, 16)
                with nc.allow_non_contiguous_dma(reason="small, once"):
                    sp.dma_start(query_i[:, :], A["positions"].rearrange("b (t p) -> p (b t)", p=P)).then_inc(here, 16)

            @block.vector
            def _(dve):
                dve.wait_ge(here, 32)
                dve.tensor_copy(key[:, :], key_i[:, :]).then_inc(floats, 1)
                dve.tensor_copy(query[:, :], query_i[:, :]).then_inc(floats, 1)
                dve.wait_ge(floats, 2)
                for t in range(TILES):
                    at, width = causal_at(t), (t + 1) * P
                    dve.tensor_scalar(near[:, at:at + width], key[:, 0:width], query[:, t:t + 1], None,
                                      ALU.subtract).then_inc(dist, 1)
                    dve.tensor_scalar(near_cmp[:, t, :], key[:, ends][:, 0:N_CMP], query[:, t:t + 1], None,
                                      ALU.subtract).then_inc(dist, 1)
                    first = max(t + 1 - WIN_BLOCKS, 0) * P
                    dve.tensor_scalar(window[:, t, 0:width - first], key[:, first:width], query[:, t:t + 1], None,
                                      ALU.subtract).then_inc(dist, 1)

            @block.gpsimd
            def _(pool):
                mine = Own(pool, own)

                def hide(ap, base, pattern, fill, per_row=1):
                    mine.link(pool.affine_select(out=ap, in_=ap, compare_op=ALU.is_ge, fill=fill, base=base,
                                                 pattern=pattern, channel_multiplier=per_row))

                for h in range(NSA_HEADS):
                    mine.link(pool.memset(slopes[:, h, 0:1], SLOPES[h]))
                    mine.link(pool.memset(slopes[:, h, 1:2], -SLOPES[h]))
                mine.link(pool.memset(fixed[:, :, :], 0.0))
                mine.link(pool.memset(seen_cmp[:, :], 1.0))
                blocks = [[P, TILES], [-SLC_BLOCK, N_SLC]]
                hide(fixed[:, :, :], -2 * SLC_BLOCK, blocks, FORCE_SCORE)
                hide(fixed[:, :, :], 0, blocks, -1.0)
                mine.link(pool.memset(fixed[:, :, 0:1], FORCE_SCORE))
                hide(seen_cmp[:, :], -(CMP_BLOCK - 1), [[-CMP_STRIDE, N_CMP]], 0.0)
                for t in range(TILES):
                    pool.wait_ge(dist, 3 * (t + 1))
                    at, width = causal_at(t), (t + 1) * P
                    hide(near[:, at + width - P:at + width], 0, [[-1, P]], -BIG)
                    first = max(t + 1 - WIN_BLOCKS, 0) * P
                    hide(window[:, t, 0:width - first], t * P - first, [[-1, width - first]], -BIG)
                    hide(window[:, t, 0:width - first], WINDOW - 1 - t * P + first, [[1, width - first]], -BIG, -1)
                hide(near_cmp[:, :, :], -(CMP_BLOCK - 1), [[P, TILES], [-CMP_STRIDE, N_CMP]], -BIG)
                mine.link(pool.tensor_copy(free[:, :, :], fixed[:, :, :]))

        with nc.Block() as block:
            @block.vector
            def _(dve):
                dve.tensor_scalar(free[:, :, :], fixed[:, :, :], 0.0, None, ALU.is_equal)


def compressed(nc, g, q_cols, k_cmp_cols, v_cmp_rows, near_cmp, seen_cmp, fixed, free, slopes, gates, near, chosen,
               o_all, ident):
    TURNS = GROUP_HEADS // 2
    W = N_CMP
    PAD = 68
    SHAPE = (P, TILES, W)
    with Phase(nc, f"cmpatt{g}") as ph:
        q = ph.sb("q", [P, SEQ])
        slope = ph.sb("slope", [P, 2, 2])
        gate = ph.sb("gate", [P, 2, BRANCHES, TILES])
        p = ph.sb("p", [P, TILES, 2, HD])
        p_cols = ph.sb("p_cols", [P, TILES, P])
        p_sum = ph.sb("p_sum", [P, TILES, PAD])
        top = ph.sb("top", [P, 2, TILES])
        total = ph.sb("total", [P, 2, TILES])
        fours = ph.sb("fours", [P, TILES, PAD // 4])
        score = ph.sb("score", [P, TILES, N_SLC])
        best = ph.sb("best", [P, TILES, 8])
        rest = ph.sb("rest", [P, TILES, N_SLC])
        s_ps = [ph.ps(f"s_ps{i}") for i in range(2)]
        t_ps = [ph.ps(f"t_ps{i}") for i in range(2)]
        o_ps = [ph.ps(f"o_ps{i}") for i in range(2)]
        (cleared, staged, scored, own, shifted, exped, p_ready, added, turned, copied, valued, out_ready, own2) = (
            ph.sem(n) for n in ("cleared", "staged", "scored", "own", "shifted", "exped", "p_ready", "added",
                                "turned", "copied", "valued", "out_ready", "own2"))
        with nc.Block() as block:
            @block.gpsimd
            def _(pool):
                pool.memset(p_sum[:, :, :], 0.0).then_inc(cleared, 1)
                pool.memset(p[:, :, :, :], 0.0).then_inc(cleared, 1)
                pool.wait_ge(cleared, 2)
                pool.sem_inc(added, 1)
                with pool.Fori(0, TURNS) as i:
                    pool.wait_ge(scored, i * 2 + 1)
                    pool.wait_ge(out_ready, i * 2 + 1)
                    pair = i + g * TURNS
                    pool.tensor_copy(q[:, :], q_cols[:, bass.ds(pair * SEQ, SEQ)]).then_inc(staged, 1)
                    pool.tensor_copy(slope[:, :, :].rearrange("p h s -> p (h s)"),
                                     slopes[:, :, :].rearrange("p h s -> p (h s)")[:, bass.ds(pair * 4, 4)]).then_inc(staged, 1)
                    pool.tensor_copy(gate[:, :, :, :].rearrange("p h r t -> p (h r t)"),
                                     gates[:, :, :, :].rearrange("p h r t -> p (h r t)")[
                                         :, bass.ds(pair * (2 * BRANCHES * TILES), 2 * BRANCHES * TILES)]).then_inc(staged, 1)
                    for h in range(2):
                        pool.wait_ge(p_ready, i * 2 + (h + 1))
                        pool.wait_ge(added, i * 2 + (h + 1))
                        pool.tensor_tensor(p_sum[:, :, 1:W + 1], p_sum[:, :, 1:W + 1], p[:, :, h, 0:W], ALU.add).then_inc(added, 1)

            @block.tensor
            def _(pe):
                pe.sem_inc(scored, 1)
                with pe.Fori(0, TURNS) as i:
                    pe.wait_ge(staged, i * 3 + 3)
                    pe.wait_ge(out_ready, i * 2 + 1)
                    for h in range(2):
                        rows = slice(h * HD, (h + 1) * HD)
                        for t in range(TILES):
                            last = pe.matmul(s_ps[h][:, t * W:(t + 1) * W], q[rows, t * P:(t + 1) * P],
                                             k_cmp_cols[rows, g, 0:W], start=True, stop=True)
                        last.then_inc(scored, 1)
                    pe.wait_ge(p_ready, i * 2 + 2)
                    for t in range(TILES):
                        last = pe.transpose(t_ps[t // 4][:, t % 4 * P:(t % 4 + 1) * P],
                                            p[:, t, :, :].rearrange("p h w -> p (h w)"), ident[:, :])
                        if t % 4 == 3:
                            last.then_inc(turned, 1)
                    pe.wait_ge(copied, i * 2 + 2)
                    for h in range(2):
                        rows = slice(h * HD, h * HD + W)
                        for t in range(TILES):
                            last = pe.matmul(o_ps[h][:, t * HD:(t + 1) * HD], p_cols[rows, t, :], v_cmp_rows[rows, g, :],
                                             start=True, stop=True)
                        last.then_inc(valued, 1)

            @block.scalar
            def _(act):
                with act.Fori(0, TURNS) as i:
                    for h in range(2):
                        act.wait_ge(shifted, i * 2 + (h + 1))
                        act.activation(p[:, :, h, 0:W], p[:, :, h, 0:W], ACT.Exp, scale=slope[:, h, 0:1]).then_inc(exped, 1)
                    for n in range(2):
                        act.wait_ge(turned, i * 2 + (n + 1))
                        act.activation(p_cols[:, 4 * n:4 * n + 4, :].rearrange("p t n -> p (t n)"), t_ps[n][:, :],
                                       ACT.Copy).then_inc(copied, 1)

            @block.vector
            def _(dve):
                dve.sem_inc(out_ready, 1)
                with dve.Fori(0, TURNS) as i:
                    step = Turn(dve, own, i, 12)
                    dve.wait_ge(cleared, 2)
                    dve.wait_ge(added, i * 2 + 1)
                    for h in range(2):
                        dve.wait_ge(scored, i * 2 + (h + 2))
                        step.link(dve.tensor_tensor(p[:, :, h, 0:W], s_ps[h][:, 0:TILES * W].rearrange("p (t w) -> p t w", t=TILES),
                                                    near_cmp[:, :, :], ALU.add))
                        step.link(dve.tensor_reduce(top[:, h, :], p[:, :, h, 0:W], X_AXIS, ALU.max))
                        dve.tensor_tensor(p[:, :, h, 0:W], p[:, :, h, 0:W], over(top[:, h, :].unsqueeze(2), SHAPE), ALU.subtract).then_inc(shifted, 1)
                    for h in range(2):
                        dve.wait_ge(exped, i * 2 + (h + 1))
                        step.link(dve.tensor_tensor(p[:, 0, h, 0:W], p[:, 0, h, 0:W], seen_cmp[:, :], ALU.mult))
                        step.link(dve.tensor_reduce(total[:, h, :], p[:, :, h, 0:W], X_AXIS, ALU.add))
                        step.link(dve.tensor_scalar(total[:, h, :], total[:, h, :], 1e-20, None, ALU.max))
                        step.link(dve.reciprocal(total[:, h, :], total[:, h, :]))
                        dve.tensor_tensor(p[:, :, h, 0:W], p[:, :, h, 0:W], over(total[:, h, :].unsqueeze(2), SHAPE), ALU.mult).then_inc(p_ready, 1)
                    assert step.n == 12
                    for h in range(2):
                        dve.wait_ge(valued, i * 2 + (h + 1))
                        to = o_all[:, bass.ds((i + g * TURNS) * SEQ, SEQ)].rearrange("p (t n) -> p t n", t=TILES)
                        dve.tensor_tensor(to[:, :, h * HD:(h + 1) * HD], o_ps[h][:, :].rearrange("p (t d) -> p t d", t=TILES),
                                          over(gate[:, h, 0, :].unsqueeze(2), (P, TILES, HD)), ALU.mult).then_inc(out_ready, 1)
                mine = Own(dve, own2)
                dve.wait_ge(added, 2 * TURNS + 1)
                mine.link(dve.tensor_reduce(fours[:, :, :], p_sum[:, :, :].rearrange("p t (j n) -> p t j n", n=4), X_AXIS, ALU.add))
                mine.link(dve.tensor_tensor(score[:, :, :], fours[:, :, 0:N_SLC], p_sum[:, :, 4:4 + 4 * (N_SLC - 1) + 1:4], ALU.add))
                mine.link(dve.tensor_tensor(score[:, :, :], score[:, :, :], free[:, :, :], ALU.mult))
                mine.link(dve.tensor_tensor(score[:, :, :], score[:, :, :], fixed[:, :, :], ALU.add))
                for t in range(TILES):
                    dve.max(best[:, t, :], score[:, t, :]).then_inc(own2, 1)
                mine.n += TILES
                dve.wait_ge(own2, mine.n)
                for t in range(TILES):
                    dve.match_replace(rest[:, t, :], best[:, t, :], score[:, t, :], -BIG).then_inc(own2, 1)
                mine.n += TILES
                dve.wait_ge(own2, mine.n)
                mine.link(dve.tensor_tensor(rest[:, :, :], rest[:, :, :], score[:, :, :], ALU.is_equal))
                mine.link(dve.tensor_scalar(rest[:, :, :], rest[:, :, :], -BIG, None, ALU.mult))
                for t in range(TILES):
                    at, n = causal_at(t), (t + 1) * P // SLC_BLOCK
                    dve.tensor_tensor(chosen[:, at:at + n * SLC_BLOCK].rearrange("p (j k) -> p j k", j=n),
                                      near[:, at:at + n * SLC_BLOCK].rearrange("p (j k) -> p j k", j=n),
                                      over(rest[:, t, 0:n].unsqueeze(2), (P, n, SLC_BLOCK)), ALU.add)


def nsa_attention(nc, g, q_cols, k_cols, v_rows, chosen, window, slopes, gates, o_all, ident):
    TURNS = GROUP_HEADS // 2
    with Phase(nc, f"nsa{g}") as ph:
        q = ph.sb("q", [P, SEQ])
        slope = ph.sb("slope", [P, 2, 2])
        gate = ph.sb("gate", [P, 2, BRANCHES, TILES])
        units = []
        for h in range(2):
            rows = slice(h * HD, (h + 1) * HD)
            for t in range(TILES):
                first = max(t + 1 - WIN_BLOCKS, 0)
                at = causal_at(t)
                common = dict(head=h, tile=t, q=q[rows, t * P:(t + 1) * P])
                units.append(dict(common, blocks=t + 1, mask=chosen[:, at:at + (t + 1) * P],
                                  k=lambda lo, hi, rows=rows: k_cols[rows, g, lo:hi],
                                  v=lambda b: v_rows[:, b, 0, g * HD:(g + 1) * HD], gate=gate[:, h, 1, t:t + 1],
                                  add=lambda i, h=h, t=t: o_all[:, bass.ds((i + g * TURNS) * SEQ + (t * P + h * HD), HD)]))
                units.append(dict(common, blocks=t + 1 - first, mask=window[:, t, 0:(t + 1 - first) * P],
                                  k=lambda lo, hi, rows=rows, first=first: k_cols[rows, KV_GROUPS + g, first * P + lo:first * P + hi],
                                  v=lambda b, first=first: v_rows[:, first + b, 1, g * HD:(g + 1) * HD],
                                  gate=gate[:, h, 2, t:t + 1], add=None))
        gates_flat = gates[:, :, :, :].rearrange("p h r t -> p (h r t)")
        slopes_flat = slopes[:, :, :].rearrange("p h s -> p (h s)")
        each = BRANCHES * TILES
        stages = [[
            (q[h * HD:(h + 1) * HD, :], lambda i, h=h: q_cols[h * HD:(h + 1) * HD, bass.ds((i + g * TURNS) * SEQ, SEQ)], "scores"),
            (gate[:, h].rearrange("p r t -> p (r t)"),
             lambda i, h=h: gates_flat[:, bass.ds((i + g * TURNS) * (2 * each) + h * each, each)], "out"),
            (slope[:, h, :], lambda i, h=h: slopes_flat[:, bass.ds((i + g * TURNS) * 4 + 2 * h, 2)], "out"),
        ] for h in range(2)]

        def scale_of(u, sign):
            return slope[:, u["head"], 0:1] if sign > 0 else slope[:, u["head"], 1:2]

        attend(nc, f"nsaatt{g}", TURNS, units, stages, scale_of, o_all, ident, g * TURNS)


def layer1(nc, A, x_rows, ident, x_dram):
    q_cols = x_rows
    x_view = x_dram.rearrange("(t p) d -> p t d", p=P)
    with Phase(nc, "layer1") as ph:
        k_cols = ph.sb("k_cols", [P, 2 * KV_GROUPS, SEQ])
        v_rows = ph.sb("v_rows", [P, TILES, 2, KV_WIDTH])
        gates = ph.sb("gates", [P, NSA_HEADS, BRANCHES, TILES])
        k_cmp_cols = ph.sb("k_cmp_cols", [P, KV_GROUPS, HD])
        v_cmp_rows = ph.sb("v_cmp_rows", [P, KV_GROUPS, HD])
        with Phase(nc, "l1a") as early:
            cmp_cols = early.sb("cmp_cols", [P, 2, SEQ])
            with Phase(nc, "l1b") as first:
                h_cols = first.sb("h_cols", [P, CHUNKS, SEQ])
                w_in = first.sb("w_in", [P, CHUNKS, NSA_IN])
                w_here, x_kept = first.sem("w_here"), first.sem("x_kept")
                nc.sync.dma_start(x_view, x_rows[:, :, :]).then_inc(x_kept, 16)
                nc.sync.dma_start(w_in[:, :, :], A["nsa_w_in"][0].rearrange("(p c) n -> p c n", p=P)).then_inc(w_here, 16)
                norm_columns(nc, "norm1", x_rows, A["norm_mix"][1], ident, h_cols)
                for eng in (nc.sync, nc.scalar, nc.vector):
                    eng.wait_ge(x_kept, 16)
                nsa_inputs(nc, h_cols, w_in, w_here, q_cols, k_cols, v_rows, cmp_cols, gates, ident, A)
            compress(nc, cmp_cols, k_cmp_cols, v_cmp_rows, ident, A)
        o_all = ph.sb("o_all", [P, PAIRS * SEQ])
        with Phase(nc, "l1c") as mid:
            near = mid.sb("near", [P, CAUSAL_WIDTH])
            chosen = mid.sb("chosen", [P, CAUSAL_WIDTH])
            window = mid.sb("window", [P, TILES, WIN_BLOCKS * P])
            near_cmp = mid.sb("near_cmp", [P, TILES, N_CMP])
            seen_cmp = mid.sb("seen_cmp", [P, N_CMP])
            fixed = mid.sb("fixed", [P, TILES, N_SLC])
            free = mid.sb("free", [P, TILES, N_SLC])
            slopes = mid.sb("slopes", [P, NSA_HEADS, 2])
            nsa_masks(nc, near, window, near_cmp, seen_cmp, fixed, free, slopes, A)
            q_flat = q_cols[:, :, :].rearrange("p c n -> p (c n)")
            for g in range(KV_GROUPS):
                compressed(nc, g, q_flat, k_cmp_cols, v_cmp_rows, near_cmp, seen_cmp, fixed, free, slopes, gates,
                           near, chosen, o_all, ident)
                nsa_attention(nc, g, q_flat, k_cols, v_rows, chosen, window, slopes, gates, o_all, ident)
        x_back = ph.sem("x_back")
        nc.sync.dma_start(x_rows[:, :, :], x_view).then_inc(x_back, 16)
        nc.vector.wait_ge(x_back, 16)
        project_out(nc, "out1", o_all[:, :].rearrange("p (c n) -> p c n", c=CHUNKS),
                    A["nsa_w_out"][0].rearrange("(c p) n -> p c n", p=P), x_rows)
def layer0(nc, A, x_rows, ident, ones, rows_to_clear):
    with Phase(nc, "layer0") as ph:
        o_cols = ph.sb("o_cols", [P, CHUNKS * SEQ])
        o_view = o_cols[:, :].rearrange("p (c n) -> p c n", c=CHUNKS)
        latents = o_cols[:, 0:TILES * LATENT].rearrange("p (t n) -> p t n", t=TILES)
        with Phase(nc, "l0a") as inner:
            conv_out = inner.sb("conv_out", [P, CONV_TILES, SEQ])
            with Phase(nc, "l0b") as early:
                h_cols = early.sb("h_cols", [P, CHUNKS, SEQ])
                w_in = early.sb("w_in", [P, CHUNKS, MIX0_IN])
                w_here = early.sem("w_here")
                nc.sync.dma_start(w_in[:, :, :], A["mix0_w_in"][0].rearrange("(p c) n -> p c n", c=CHUNKS)).then_inc(w_here, 16)
                norm_columns(nc, "norm0", x_rows, A["norm_mix"][0], ident, h_cols)
                mix0_input(nc, h_cols, w_in, w_here, latents, conv_out, A)
            conv_norm(nc, conv_out, ones, o_view, A)
        q_cols = ph.sb("q_cols", [P, MLA_HEADS, SEQ])
        k_cols = ph.sb("k_cols", [P, MLA_HEADS, SEQ])
        v_rows = ph.sb("v_rows", [P, TILES, MLA_HEADS * V_DIM])
        mla_inputs(nc, latents, q_cols, k_cols, v_rows, ident, A)
        mla_attention(nc, q_cols[:, :, :].rearrange("p h n -> p (h n)"), k_cols[:, :, :].rearrange("p h n -> p (h n)"),
                      v_rows, o_cols, ident, rows_to_clear)
        project_out(nc, "out0", o_view, A["mix0_w_out"][0].rearrange("(c p) n -> p c n", p=P), x_rows)


def trunk(nc, A, out):
    scratch = (nc.dram_tensor("h_rows", (SEQ, D), F32).ap(), nc.dram_tensor("y_rows", (BLOCKS * P, D), F32).ap(),
               nc.dram_tensor("row_token", (BLOCKS * P, 1), I32).ap())
    x_dram = nc.dram_tensor("x_kept", (SEQ, D), F32).ap()
    Phase.numbers.clear()
    pool_sems = [pool_semaphores(nc, layer) for layer in range(2)]
    with Phase(nc, "trunk") as ph:
        x_rows = ph.sb("x_rows", [P, TILES, D])
        ident = ph.sb("ident", [P, P])
        ones = ph.sb("ones", [P, P])
        constants(nc, x_rows, ident, ones, A)
        layer0(nc, A, x_rows, ident, ones, scratch[1][EXPERTS * P:, :])
        moe(nc, 0, x_rows, ident, ones, scratch, pool_sems[0], A)
        clear_semaphores(nc)
        layer1(nc, A, x_rows, ident, x_dram)
        clear_semaphores(nc)
        moe(nc, 1, x_rows, ident, ones, scratch, pool_sems[1], A)
        store_rows(nc, x_rows, out)


NAMES = ["x", "positions", "norm_mix", "norm_ffn", "mix0_w_in", "mla_q_a_norm", "mla_w_uq", "mla_kv_a_norm",
         "mla_w_ukv", "mla_q_norm", "mla_k_norm", "conv_dw_w", "conv_dw_b", "conv_ln_g", "conv_ln_b", "mix0_w_out",
         "nsa_w_in", "nsa_q_norm", "nsa_k_norm_cmp", "nsa_k_norm_slc", "nsa_k_norm_win", "nsa_cmp_pe_k",
         "nsa_cmp_w1_k", "nsa_cmp_w2_k", "nsa_cmp_pe_v", "nsa_cmp_w1_v", "nsa_cmp_w2_v", "nsa_w_out",
         "moe_router_group", "moe_router_group_b", "moe_router_expert", "moe_router_expert_b",
         "moe_w_gate", "moe_w_up", "moe_w_down"]


def kernel(**inputs):
    import concourse.bacc as _bacc
    from concourse.bass_utils import run_bass_kernel_spmd as _run

    nc = _bacc.Bacc("TRN2", target_bir_lowering=False, num_devices=1)
    arrays, args = {}, {}
    for name in NAMES:
        a = np.ascontiguousarray(inputs[name])
        arrays[f"in_{name}_dram"] = a
        args[name] = nc.dram_tensor(f"in_{name}_dram", a.shape, mybir.dt.from_np(a.dtype), kind="ExternalInput").ap()
    out = nc.dram_tensor("out_0_dram", (1, SEQ, D), F32, kind="ExternalOutput").ap()
    trunk(nc, args, out)
    r = _run(nc, [arrays], core_ids=[0])
    return r.results[0]["out_0_dram"]
```
